# Optimizing a Trainium2 kernel written in Bass

```python
import math
import jax, jax.numpy as jnp
from jax import lax
import numpy as np

'''Two trunk layers of a hybrid diffusion / flow-matching backbone with a context prefix.

Layer pattern: even layers = [Conformer conv module || differential attention] as parallel
head groups behind one combined input projection and one output projection; odd layers =
[multi-scale pooling mixer || short gated convolution mixer] likewise; every layer is followed
by a hierarchical (top-1 group, then top-2 expert) MoE of gated MLPs. Pre-RMSNorm, adaLN
shift/scale/gate from SiLU(cond) per sub-layer, plain residual adds, one final RMSNorm.
Context tokens are modulated by c_ctx and read only context tokens; latent tokens read
context keys/values (attention only) plus all latent tokens.

Inputs:
  x_prompt (BATCH, SEQ, D_MODEL)            context tokens of new requests
  x_sample (DEC_BATCH, DEC_SEQ, D_MODEL)    noisy latent tokens (grid of width GRID_W)
  cache_k  (DEC_BATCH, N_ATTN_LAYERS, PAST_LEN, DIFF_HEADS, 2, DIFF_DH)  cached context keys
  cache_v  (DEC_BATCH, N_ATTN_LAYERS, PAST_LEN, DIFF_HEADS, 2*DIFF_DH)   cached context values
  c        (DEC_BATCH, D_MODEL)             conditioning of denoising requests
  c_ctx    (D_MODEL,)                       learned context conditioning vector
  followed by the weights.
Output tuple:
  y_prompt    (BATCH, SEQ, D_MODEL)
  y_sample    (DEC_BATCH, DEC_SEQ, D_MODEL)
  new_cache_k (BATCH, N_ATTN_LAYERS, SEQ, DIFF_HEADS, 2, DIFF_DH)
  new_cache_v (BATCH, N_ATTN_LAYERS, SEQ, DIFF_HEADS, 2*DIFF_DH)
'''

D_MODEL = 1024
BATCH = 1
SEQ = 128
DEPTH = 2
DEC_BATCH = 1
DEC_SEQ = 512
PAST_LEN = 128

GRID_W = 64
MIX_W = D_MODEL
HALF_W = MIX_W // 2
CONV_CH = HALF_W
CONV_K = 31
DIFF_HEADS = 4
DIFF_DH = HALF_W // (2 * DIFF_HEADS)
QK_W = DIFF_HEADS * 2 * DIFF_DH
AX_DIM = DIFF_DH // 2
ROPE_BASE = 10000.0
POOL_WINDOWS = (2, 4, 8, 16)
POOL_CH = HALF_W
POOL_GC = POOL_CH // len(POOL_WINDOWS)
SCONV_CH = HALF_W
SCONV_K = 3
N_GROUPS = 4
EXPERTS_PER_GROUP = 8
N_EXPERTS = N_GROUPS * EXPERTS_PER_GROUP
TOP_K = 2
EXPERT_HIDDEN = D_MODEL // 2
MOE_BLOCK = 128
Q_BLOCK = 128
N_EVEN = (DEPTH + 1) // 2
N_ODD = DEPTH // 2
N_ATTN_LAYERS = N_EVEN
EVEN_IN = 2 * CONV_CH + 3 * QK_W
ODD_IN = POOL_CH + 3 * SCONV_CH
EPS = 1e-6

kernel_name = 'hybrid_prefix_diffusion_step'

def rmsnorm(x, g):
    xf = x.astype(jnp.float32)
    y = xf * lax.rsqrt(jnp.mean(xf * xf, axis=-1, keepdims=True) + EPS)
    return (y * g.astype(jnp.float32)).astype(x.dtype)

def layernorm(x, g, b):
    xf = x.astype(jnp.float32)
    mu = jnp.mean(xf, axis=-1, keepdims=True)
    var = jnp.mean(jnp.square(xf - mu), axis=-1, keepdims=True)
    y = (xf - mu) * lax.rsqrt(var + EPS)
    return (y * g.astype(jnp.float32) + b.astype(jnp.float32)).astype(x.dtype)

def dwconv(x, w):
    k = w.shape[0]
    pad = k // 2
    return lax.conv_general_dilated(x, w[:, None, :].astype(x.dtype), window_strides=(1,),
                                    padding=[(pad, pad)], dimension_numbers=('NWC', 'WIO', 'NWC'),
                                    feature_group_count=x.shape[-1])

def axial_rope_tables(t_len):
    rows = t_len // GRID_W
    row = jnp.repeat(jnp.arange(rows, dtype=jnp.float32), GRID_W)
    col = jnp.tile(jnp.arange(GRID_W, dtype=jnp.float32), rows)
    inv = ROPE_BASE ** (-jnp.arange(0, AX_DIM, 2, dtype=jnp.float32) / AX_DIM)
    ar = row[:, None] * inv[None, :]
    ac = col[:, None] * inv[None, :]
    return (jnp.cos(ar), jnp.sin(ar), jnp.cos(ac), jnp.sin(ac))

def _rot(x, cos, sin):
    h = x.shape[-1] // 2
    x1, x2 = x[..., :h], x[..., h:]
    return jnp.concatenate([x1 * cos - x2 * sin, x1 * sin + x2 * cos], axis=-1)

def axial_rope(x, tables):
    cr, sr, cc, sc = [t[None, :, None, None, :].astype(x.dtype) for t in tables]
    return jnp.concatenate([_rot(x[..., :AX_DIM], cr, sr), _rot(x[..., AX_DIM:], cc, sc)], axis=-1)

def diff_attention(q, k, v, lam):
    b, t, h, _, dh = q.shape
    qb_len = min(Q_BLOCK, t)
    nq = t // qb_len
    qb = jnp.moveaxis(q.reshape(b, nq, qb_len, h, 2, dh), 1, 0)
    scale = dh ** -0.5

    def block(qblk):
        s = jnp.einsum('bqhcd,bkhcd->bhcqk', qblk, k).astype(jnp.float32) * scale
        pr = jax.nn.softmax(s, axis=-1)
        a = (pr[:, :, 0] - lam * pr[:, :, 1]).astype(v.dtype)
        return jnp.einsum('bhqk,bkhe->bqhe', a, v)

    o = lax.map(block, qb)
    return jnp.moveaxis(o, 0, 1).reshape(b, t, h, 2 * dh)

def multiscale_pool(xc, w_grp, scale):
    b, t, _ = xc.shape
    ng = len(POOL_WINDOWS)
    xg = xc.reshape(b, t, ng, POOL_GC).astype(jnp.float32)
    cs = jnp.concatenate([jnp.zeros((b, 1, ng, POOL_GC), jnp.float32), jnp.cumsum(xg, axis=1)], axis=1)
    pos = jnp.arange(t)
    outs = []
    for g, w in enumerate(POOL_WINDOWS):
        lo = jnp.maximum(pos - w // 2, 0)
        hi = jnp.minimum(pos + w // 2 - 1, t - 1)
        cnt = (hi - lo + 1).astype(jnp.float32)
        outs.append((cs[:, hi + 1, g] - cs[:, lo, g]) / cnt[None, :, None])
    d = (jnp.stack(outs, axis=2) - xg).astype(xc.dtype)
    y = jnp.einsum('btgc,gce->btge', d, w_grp).reshape(b, t, POOL_CH)
    return y * scale

def hmoe(x, w_rg, b_rg, w_re, b_re, w_g, w_u, w_d):
    n, d = x.shape
    gp = jax.nn.softmax((x @ w_rg + b_rg).astype(jnp.float32), axis=-1)
    g_idx = jnp.argmax(gp, axis=-1).astype(jnp.int32)
    g_p = jnp.take_along_axis(gp, g_idx[:, None], axis=-1)[:, 0]
    el_all = jnp.einsum('nd,gde->nge', x, w_re) + b_re
    el = jnp.take_along_axis(el_all, g_idx[:, None, None], axis=1)[:, 0].astype(jnp.float32)
    top_v, top_i = lax.top_k(el, TOP_K)
    wts = jax.nn.softmax(top_v, axis=-1) * g_p[:, None]
    eid = g_idx[:, None] * EXPERTS_PER_GROUP + top_i.astype(jnp.int32)

    a_len = n * TOP_K
    flat_e = eid.reshape(-1)
    flat_t = jnp.repeat(jnp.arange(n, dtype=jnp.int32), TOP_K)
    flat_w = wts.reshape(-1)
    order = jnp.argsort(flat_e)
    counts = jnp.zeros((N_EXPERTS,), jnp.int32).at[flat_e].add(1)
    pc = ((counts + MOE_BLOCK - 1) // MOE_BLOCK) * MOE_BLOCK
    start = jnp.cumsum(counts) - counts
    pend = jnp.cumsum(pc)
    pstart = pend - pc
    se = flat_e[order]
    dest = pstart[se] + (jnp.arange(a_len, dtype=jnp.int32) - start[se])
    p_len = a_len + N_EXPERTS * MOE_BLOCK
    nblk = p_len // MOE_BLOCK
    row_tok = jnp.full((p_len,), n, jnp.int32).at[dest].set(flat_t[order])
    row_w = jnp.zeros((p_len,), x.dtype).at[dest].set(flat_w[order].astype(x.dtype))
    blk_e = jnp.minimum(jnp.searchsorted(pend, jnp.arange(nblk, dtype=jnp.int32) * MOE_BLOCK, side='right'),
                        N_EXPERTS - 1).astype(jnp.int32)
    xp = jnp.concatenate([x, jnp.zeros((1, d), x.dtype)], axis=0)
    xb = xp[row_tok].reshape(nblk, MOE_BLOCK, d)

    def expert_block(args):
        xblk, e = args
        hid = jax.nn.silu(xblk @ w_g[e]) * (xblk @ w_u[e])
        return hid @ w_d[e]

    yb = lax.map(expert_block, (xb, blk_e)).reshape(p_len, d)
    y = jax.ops.segment_sum(yb * row_w[:, None], row_tok, num_segments=n + 1)
    return y[:n]

def even_mixer(h, p, j, i, rope, ctx_kv):
    b, t, _ = h.shape
    proj = h @ p['w_in_e'][j]
    ga, gb, q, k, v = jnp.split(proj, [CONV_CH, 2 * CONV_CH, 2 * CONV_CH + QK_W, 2 * CONV_CH + 2 * QK_W], axis=-1)
    u = ga * jax.nn.sigmoid(gb)
    u = dwconv(u, p['conv_a_w'][j]) + p['conv_a_b'][j]
    u = jax.nn.silu(layernorm(u, p['ln_a_g'][j], p['ln_a_b'][j]))
    q = q.reshape(b, t, DIFF_HEADS, 2, DIFF_DH)
    k = k.reshape(b, t, DIFF_HEADS, 2, DIFF_DH)
    v = v.reshape(b, t, DIFF_HEADS, 2 * DIFF_DH)
    if rope is not None:
        q = axial_rope(q, rope)
        k = axial_rope(k, rope)
    if ctx_kv is None:
        keys, vals = k, v
    else:
        keys = jnp.concatenate([ctx_kv[0].astype(k.dtype), k], axis=1)
        vals = jnp.concatenate([ctx_kv[1].astype(v.dtype), v], axis=1)
    lam_init = 0.8 - 0.6 * math.exp(-0.3 * i)
    f32 = jnp.float32
    lam = (jnp.exp(jnp.sum(p['lam_q1'][j].astype(f32) * p['lam_k1'][j].astype(f32)))
           - jnp.exp(jnp.sum(p['lam_q2'][j].astype(f32) * p['lam_k2'][j].astype(f32))) + lam_init)
    o = diff_attention(q, keys, vals, lam)
    o = rmsnorm(o, p['subln_g'][j]) * (1.0 - lam_init)
    out = jnp.concatenate([u, o.reshape(b, t, QK_W)], axis=-1) @ p['w_out_e'][j]
    return out, k, v

def odd_mixer(h, p, j):
    proj = h @ p['w_in_o'][j]
    xc, hd, bg, cg = jnp.split(proj, [POOL_CH, POOL_CH + SCONV_CH, POOL_CH + 2 * SCONV_CH], axis=-1)
    yc = multiscale_pool(xc, p['pool_w'][j], p['pool_scale'][j])
    yd = bg * dwconv(cg * hd, p['conv_d_w'][j])
    return jnp.concatenate([yc, yd], axis=-1) @ p['w_out_o'][j]

def run_trunk(x, cond, p, rope, ctx_k, ctx_v):
    new_k, new_v = [], []
    for i in range(DEPTH):
        j = i // 2
        mod = (cond @ p['w_ada'][i] + p['b_ada'][i])[:, None, :]
        sh1, sc1, g1, sh2, sc2, g2 = jnp.split(mod, 6, axis=-1)
        h = rmsnorm(x, p['g_norm1'][i]) * (1 + sc1) + sh1
        if i % 2 == 0:
            kv_in = None if ctx_k is None else (ctx_k[:, j], ctx_v[:, j])
            m, k_cur, v_cur = even_mixer(h, p, j, i, rope, kv_in)
            if ctx_k is None:
                new_k.append(k_cur)
                new_v.append(v_cur)
        else:
            m = odd_mixer(h, p, j)
        x = x + g1 * m
        h = rmsnorm(x, p['g_norm2'][i]) * (1 + sc2) + sh2
        b, t, d = h.shape
        y = hmoe(h.reshape(b * t, d), p['w_router_g'][i], p['b_router_g'][i], p['w_router_e'][i],
                 p['b_router_e'][i], p['w_gate'][i], p['w_up'][i], p['w_down'][i])
        x = x + g2 * y.reshape(b, t, d)
    return rmsnorm(x, p['g_final']), new_k, new_v

def setup_inputs(seed: int = 0) -> dict:
    key = jax.random.key(seed)
    ks = iter(jax.random.split(key, 40))
    D = D_MODEL

    def nrm(shape, s=1.0):
        return jax.random.normal(next(ks), shape, jnp.float32) * s

    def gain(shape):
        return 1.0 + nrm(shape, 0.02)

    return {
        'x_prompt': nrm((BATCH, SEQ, D)),
        'x_sample': nrm((DEC_BATCH, DEC_SEQ, D)),
        'cache_k': nrm((DEC_BATCH, N_ATTN_LAYERS, PAST_LEN, DIFF_HEADS, 2, DIFF_DH)),
        'cache_v': nrm((DEC_BATCH, N_ATTN_LAYERS, PAST_LEN, DIFF_HEADS, 2 * DIFF_DH)),
        'c': nrm((DEC_BATCH, D)),
        'c_ctx': nrm((D,)),
        'w_ada': nrm((DEPTH, D, 6 * D), 0.5 * D ** -0.5),
        'b_ada': nrm((DEPTH, 6 * D), 0.02),
        'g_norm1': gain((DEPTH, D)),
        'g_norm2': gain((DEPTH, D)),
        'g_final': gain((D,)),
        'w_in_e': nrm((N_EVEN, D, EVEN_IN), D ** -0.5),
        'conv_a_w': nrm((N_EVEN, CONV_K, CONV_CH), CONV_K ** -0.5),
        'conv_a_b': nrm((N_EVEN, CONV_CH), 0.02),
        'ln_a_g': gain((N_EVEN, CONV_CH)),
        'ln_a_b': nrm((N_EVEN, CONV_CH), 0.02),
        'lam_q1': nrm((N_EVEN, DIFF_DH), 0.1),
        'lam_k1': nrm((N_EVEN, DIFF_DH), 0.1),
        'lam_q2': nrm((N_EVEN, DIFF_DH), 0.1),
        'lam_k2': nrm((N_EVEN, DIFF_DH), 0.1),
        'subln_g': gain((N_EVEN, 2 * DIFF_DH)),
        'w_out_e': nrm((N_EVEN, MIX_W, D), MIX_W ** -0.5),
        'w_in_o': nrm((N_ODD, D, ODD_IN), D ** -0.5),
        'pool_w': nrm((N_ODD, len(POOL_WINDOWS), POOL_GC, POOL_GC), POOL_GC ** -0.5),
        'pool_scale': gain((N_ODD, POOL_CH)),
        'conv_d_w': nrm((N_ODD, SCONV_K, SCONV_CH), SCONV_K ** -0.5),
        'w_out_o': nrm((N_ODD, MIX_W, D), MIX_W ** -0.5),
        'w_router_g': nrm((DEPTH, D, N_GROUPS), D ** -0.5),
        'b_router_g': nrm((DEPTH, N_GROUPS), 0.01),
        'w_router_e': nrm((DEPTH, N_GROUPS, D, EXPERTS_PER_GROUP), D ** -0.5),
        'b_router_e': nrm((DEPTH, N_GROUPS, EXPERTS_PER_GROUP), 0.01),
        'w_gate': nrm((DEPTH, N_EXPERTS, D, EXPERT_HIDDEN), D ** -0.5),
        'w_up': nrm((DEPTH, N_EXPERTS, D, EXPERT_HIDDEN), D ** -0.5),
        'w_down': nrm((DEPTH, N_EXPERTS, EXPERT_HIDDEN, D), EXPERT_HIDDEN ** -0.5),
    }

def reference(x_prompt, x_sample, cache_k, cache_v, c, c_ctx, w_ada, b_ada, g_norm1, g_norm2, g_final,
              w_in_e, conv_a_w, conv_a_b, ln_a_g, ln_a_b, lam_q1, lam_k1, lam_q2, lam_k2, subln_g, w_out_e,
              w_in_o, pool_w, pool_scale, conv_d_w, w_out_o, w_router_g, b_router_g, w_router_e, b_router_e,
              w_gate, w_up, w_down):
    p = {
        'w_ada': w_ada, 'b_ada': b_ada, 'g_norm1': g_norm1, 'g_norm2': g_norm2, 'g_final': g_final,
        'w_in_e': w_in_e, 'conv_a_w': conv_a_w, 'conv_a_b': conv_a_b, 'ln_a_g': ln_a_g, 'ln_a_b': ln_a_b,
        'lam_q1': lam_q1, 'lam_k1': lam_k1, 'lam_q2': lam_q2, 'lam_k2': lam_k2, 'subln_g': subln_g,
        'w_out_e': w_out_e, 'w_in_o': w_in_o, 'pool_w': pool_w, 'pool_scale': pool_scale,
        'conv_d_w': conv_d_w, 'w_out_o': w_out_o, 'w_router_g': w_router_g, 'b_router_g': b_router_g,
        'w_router_e': w_router_e, 'b_router_e': b_router_e, 'w_gate': w_gate, 'w_up': w_up, 'w_down': w_down,
    }
    y_prompt, new_k, new_v = run_trunk(x_prompt, jax.nn.silu(c_ctx)[None, :], p, None, None, None)
    new_cache_k = jnp.stack(new_k, axis=1)
    new_cache_v = jnp.stack(new_v, axis=1)
    rope = axial_rope_tables(x_sample.shape[1])
    y_sample, _, _ = run_trunk(x_sample, jax.nn.silu(c), p, rope, cache_k, cache_v)
    return (y_prompt, y_sample, new_cache_k, new_cache_v)


_drawn_inputs = setup_inputs


def setup_inputs(seed=0):
    import zlib

    import numpy as np

    out = dict(_drawn_inputs(seed))
    spreads = {}
    factors = {'g_norm1': 3.009,
     'g_norm2': 3.25,
     'g_final': 8.387,
     'conv_a_b': 5.172,
     'ln_a_g': 5.564,
     'ln_a_b': 4.681,
     'lam_q2': 2.953,
     'subln_g': 5.067,
     'pool_scale': 20.334,
     'b_router_g': 7.698,
     'b_router_e': 6.704,
     'cache_k': 8.0,
     'cache_v': 8.0}
    for name, (base, spread) in spreads.items():
        noise = np.random.default_rng([zlib.crc32(name.encode()), seed]).standard_normal(out[name].shape)
        drawn = base * np.exp(spread * noise) if base else spread * noise
        out[name] = __import__('jax').numpy.asarray(drawn.astype(out[name].dtype))
    for name, factor in factors.items():
        out[name] = (out[name] * factor).astype(out[name].dtype)
    return out
```

```python
import math
from contextlib import ExitStack

import numpy as np
import concourse.bass as bass
from concourse import mybir

D, TOK, NT, DC = 1024, 640, 5, 8
NS, NP = 512, 128
HALF, HC = 512, 4
HEADS, DH, PAST = 4, 64, 128
TAPS, GRID_W, AX = 31, 64, 32
NG, EPG = 4, 8
NE = NG * EPG
HID = 512
CAP = 80
OVER = (2 * TOK) // (CAP + 1)
NBLK = NE + OVER
MORE = -(-TOK // CAP) - 1
NOROW = 65536.0
EPS = 1e-6
LAM_INIT = 0.8 - 0.6 * math.exp(-0.3 * 0)
SLOT = 4096
WINDOWS = (2, 4, 8, 16)


def shape_constants():
    inv = (np.float32(10000.0) ** (-np.arange(0, AX, 2, dtype=np.float32) / np.float32(AX))).astype(np.float32)
    pos = np.arange(NS)
    ar = (pos // GRID_W).astype(np.float32)[:, None] * inv[None]
    ac = (pos % GRID_W).astype(np.float32)[:, None] * inv[None]
    ang = np.concatenate([ar, ar, ac, ac], axis=1).T
    ang = np.concatenate([ang, ang], axis=0).astype(np.float32)
    rot = np.zeros((128, 128), np.float32)
    for m in range(128):
        if m % 32 < 16:
            rot[m + 16, m] = -1.0
        else:
            rot[m - 16, m] = 1.0
    strict = np.triu(np.ones((128, 128), np.float32), 1)
    square = np.concatenate([np.eye(128, dtype=np.float32), np.ones((128, 128), np.float32), strict, rot,
                             np.cos(ang), np.sin(ang)], axis=1)
    counts = np.zeros((HC, TOK), np.float32)
    for g, w in enumerate(WINDOWS):
        for start, n in ((0, NS), (NS, NP)):
            p = np.arange(n)
            counts[g, start:start + n] = 1.0 / (np.minimum(p + w // 2 - 1, n - 1) - np.maximum(p - w // 2, 0) + 1)
    iotas = np.concatenate([np.arange(NG) - 100, np.arange(EPG) - 100, np.arange(NE), np.arange(CAP),
                            np.arange(NBLK), np.arange(OVER)]).astype(np.float32)
    rows = np.zeros((128, 2, 2, NT), np.float32)
    tok = np.arange(NT)[None] * 128 + np.arange(128)[:, None]
    for k in range(2):
        rows[:, 0, k] = tok - NOROW
        rows[:, 1, k] = 2 * tok + k - NOROW
    return {"const_square": square, "const_counts": counts.reshape(-1), "const_iotas": iotas,
            "const_rows": rows.reshape(128, -1)}


def build(nc, a, out):
    f32, i32 = mybir.dt.float32, mybir.dt.int32
    ALU, ACT, AX_X = mybir.AluOpType, mybir.ActivationFunctionType, mybir.AxisListType.X
    SP, PE, DVE, POOL, ACTE = (mybir.EngineType.SP, mybir.EngineType.PE, mybir.EngineType.DVE,
                               mybir.EngineType.Pool, mybir.EngineType.Activation)
    ctx = ExitStack()
    with ctx:
        def sb(name, cols, dt=f32):
            return ctx.enter_context(nc.sbuf_tensor(name, [128, cols], dt))

        X = sb("x_residual", NT * D)[:, :].rearrange("p (t d) -> p t d", t=NT)
        BC = sb("gates_by_token", 4 * D)[:, :].rearrange("p (q c d) -> p q c d", q=2, c=2)
        RING = sb("weight_ring", 6 * SLOT)
        SQ = sb("square_consts", 4 * 128 + 2 * NS)
        ident, ones, strict, rot = (SQ[:, i * 128:(i + 1) * 128] for i in range(4))
        cos, sin = SQ[:, 512:512 + NS], SQ[:, 512 + NS:512 + 2 * NS]
        NIO = NG + EPG + NE + CAP + NBLK + OVER
        IO = sb("iotas", NIO)
        o = 0
        iota = {}
        for n, w in (("g", NG), ("e", EPG), ("E", NE), ("c", CAP), ("b", NBLK), ("o", OVER)):
            iota[n] = IO[:, o:o + w]
            o += w
        ROWS = sb("row_numbers", 20)[:, :].rearrange("p (s k t) -> p s k t", s=2, k=2)
        P1 = sb("params_1", 128)
        P2 = sb("params_2", 125)
        P3 = sb("params_3", 28)
        b_adaT = P1[:, 0:96].rearrange("p (l c) -> p l c", l=2)
        g_n1T = P1[:, 96:112].rearrange("p (l k) -> p l k", l=2)
        conv_bT, ln_gT, ln_bT, pool_sT = (P1[:, 112 + 4 * i:116 + 4 * i] for i in range(4))
        conv_wT = P2[:, 0:124].rearrange("p (t j) -> p t j", t=TAPS)
        sublnT = P2[:, 124:125]
        sconv_wT = P3[:, 0:12].rearrange("p (t j) -> p t j", t=3)
        g_n2T = P3[:, 12:28].rearrange("p (l k) -> p l k", l=2)
        condT = sb("cond_T", 16)
        MOD = sb("modulation_T", 2 * 96)[:, :].rearrange("p (l c s) -> p l c s", l=2, c=48)
        SC1 = sb("scale1_T", 32)[:, :].rearrange("p (l k s) -> p l k s", l=2, k=8)
        SC2 = sb("scale2_T", 32)[:, :].rearrange("p (l k s) -> p l k s", l=2, k=8)
        WR = sb("router_weights", 2 * DC * 36)[:, :].rearrange("p (l k n) -> p l k n", l=2, k=DC)
        BR = sb("router_bias", 72)[:, :].rearrange("p (l n) -> p l n", l=2)
        small = sb("small", 160)
        ssq, rstd = small[:, 0:5], small[:, 5:10]
        lam2, laml, lam_neg = small[:, 10:12], small[:, 12:14], small[:, 14:15]
        eps1 = small[:, 15:16]
        oss, orstd = small[:, 20:40], small[:, 40:60]
        smx, snb, sl, sr = (small[:, 60 + 4 * i:64 + 4 * i].rearrange("p (u c) -> p u c", u=2) for i in range(4))
        sub2 = small[:, 80:81]
        WT1, WT2 = small[:, 90:95], small[:, 95:100]
        IDX = sb("row_index_table", 2 * NBLK, i32)
        NBK = sb("further_blocks", 1 + OVER, i32)
        GI = [sb(f"gather_rows_{i}", 1, i32) for i in range(2)]
        SI = [sb(f"scatter_rows_{i}", 1, i32) for i in range(2)]
        SCR_N = 16128
        SCR = sb("scratch", SCR_N)

        def scr(at, n):
            assert at + n <= SCR_N
            return SCR[:, at:at + n]

        def slot(s):
            return RING[:, s * SLOT:(s + 1) * SLOT]

        free45 = RING[:, 4 * SLOT:6 * SLOT]
        hT = scr(0, DC * TOK).rearrange("p (k t) -> p k t", k=DC)
        XN = free45[:, 0:NT * D].rearrange("p (t d) -> p t d", t=NT)
        junk1, junk2 = scr(8400, D), scr(15104, D)
        qT = scr(5120, HC * TOK).rearrange("p (h t) -> p h t", h=HC)
        kT = scr(7680, HC * TOK).rearrange("p (h t) -> p h t", h=HC)
        V = scr(10240, NT * HALF).rearrange("p (t n) -> p t n", t=NT)
        KC = scr(12800, HALF)
        kcT = scr(13312, HALF).rearrange("p (h t) -> p h t", h=HC)
        VC = scr(13824, HALF)
        GA = scr(14336, TOK)
        SG = scr(14976, TOK)
        AT = scr(14336, 2 * TOK).rearrange("p (u t) -> p u t", u=2)
        RQ = scr(15616, NS)
        LAMV = scr(15616, 4 * DH)
        UPW, UOW = 15 * 3 + TOK, 15 + TOK
        UP = free45[:, 0:HC * UPW].rearrange("p (j w) -> p j w", j=HC)
        UO = free45[:, HC * UPW:HC * (UPW + UOW)].rearrange("p (j w) -> p j w", j=HC)
        assert HC * (UPW + UOW) + HC * TOK <= 2 * SLOT
        catU = free45[:, HC * (UPW + UOW):HC * (UPW + UOW) + HC * TOK].rearrange("p (j t) -> p j t", j=HC)
        QC = catU[:, 0, 0:NS]
        MU, RS = free45[:, 0:UOW], free45[:, UOW:2 * UOW]
        SQB = [free45[:, (2 + i) * UOW:(3 + i) * UOW] for i in range(2)]
        PR = scr(0, 4 * TOK).rearrange("p (u c t) -> p u c t", u=2, c=2)
        OR = scr(2560, NT * HALF).rearrange("p (t n) -> p t n", t=NT)
        oT = scr(5120, HC * TOK).rearrange("p (h t) -> p h t", h=HC)
        XPW = 8 * 3 + TOK
        TPW = 3 + TOK
        CNT = scr(5120, HC * TOK).rearrange("p (j t) -> p j t", j=HC)
        XP = scr(7680, XPW)
        PS2 = [scr(8400 + 700 * i, XPW) for i in range(2)]
        HD = scr(9800, TOK)
        CG = scr(10440, TOK)
        TP = scr(11080, TPW)
        CA = scr(11730, TPW)
        BG = scr(12380, TOK)
        DP = scr(13024, HC * TOK).rearrange("p (j t) -> p j t", j=HC)
        PW = scr(15584, HC * 128).rearrange("p (j e) -> p j e", j=HC)
        CAT = free45[:, 0:DC * TOK].rearrange("p (k t) -> p k t", k=DC)
        TMP = [scr(14336, 512)]
        M2 = scr(0, 4 * D).rearrange("p (q c d) -> p q c d", q=2, c=2)
        H2 = [scr(4096 + D * i, D) for i in range(2)]
        H2T = [scr(6144 + D * i, D).rearrange("p (k t) -> p k t", k=DC) for i in range(2)]
        XG = [scr(8192 + D * i, D) for i in range(2)]
        XGT = [scr(10240 + DC * CAP * i, DC * CAP) for i in range(2)]
        HIDT = [scr(11520 + HC * CAP * i, HC * CAP) for i in range(2)]
        SIL = scr(12160, HC * CAP)
        YR = [scr(12480 + D * i, D) for i in range(2)]
        POSH = scr(10240, 10 * CAP).rearrange("p (a c) -> p a c", a=10)
        VAL = scr(10240 + 10 * CAP, 10 * 2 * NBLK).rearrange("p (a s b) -> p a s b", a=10, s=2)
        RT = 14528
        BOTH_AT = RT + 25
        YB = [scr(2 * D * i, 2 * D) for i in range(2)]
        GF = scr(4096, D)

        PB = [ctx.enter_context(nc.psum_tensor(f"psum_pair_{n}", [128, 1024], f32)) for n in "ABCD"]
        A_, B_, C_, D_ = range(4)
        HALVES = PB[B_][:, :].rearrange("p (h c) -> p h c", h=2)
        h2_dram = nc.dram_tensor("h2_rows", [TOK, D], f32, kind="Internal").ap()
        y_dram = nc.dram_tensor("expert_rows", [2 * TOK, D], f32, kind="Internal").ap()

        sems = {}

        def sig(name, *at):
            key = "_".join([name, *map(str, at)])
            if key not in sems:
                sems[key] = ctx.enter_context(nc.semaphore(key))
            return sems[key]

        slot_full = [sig("slot_full", s) for s in range(6)]
        slot_free = [sig("slot_free", s) for s in range(6)]
        psum_ready = [sig("psum_ready", p) for p in range(4)]
        psum_taken = [sig("psum_taken", p) for p in range(4)]

        def ada_pages(l, lo, hi):
            w = a["w_ada"][l].rearrange("(k p) n -> p k n", p=128)
            return [(("ada", l, c), w[:, :, c * 512:(c + 1) * 512]) for c in range(lo, hi)]

        def in_pages(tag, w, n):
            w = w.rearrange("(k p) n -> p k n", p=128)
            return [((tag, c), w[:, :, c * 512:(c + 1) * 512]) for c in range(n)]

        dense = [ada_pages(0, 0, 4) + in_pages("in_e", a["w_in_e"][0], 5) + ada_pages(0, 4, 12)
                 + ada_pages(1, 0, 12) + in_pages("out_e", a["w_out_e"][0], 2),
                 in_pages("in_o", a["w_in_o"][0], 4) + in_pages("out_o", a["w_out_o"][0], 2)]
        page_at, fills, frees = {}, [0] * 6, [0] * 6
        moe_base, plan = [], []
        for l in range(2):
            for i, (name, src) in enumerate(dense[l]):
                s = i % 4
                page_at[name] = (s, fills[s] + 1)
                plan.append((l, name, src, s, frees[s]))
                fills[s] += 1
                frees[s] += 1
            moe_base.append((list(fills), list(frees)))
            fills = [f + NE // 2 for f in fills]

        def page(eng, name):
            s, n = page_at[name]
            eng.wait_ge(slot_full[s], 16 * n)
            return slot(s).rearrange("p (k n) -> p k n", k=DC)

        def free_page(ins, name):
            ins.then_inc(slot_free[page_at[name][0]], 1)

        uses, count = {}, [0] * 4

        def put(pair, *name):
            uses[name] = (pair, count[pair])
            count[pair] += 1

        def put_ab(names):
            for i, n in enumerate(names):
                put(i % 2, *n)

        UNITS = [(t, h) for t in range(4) for h in range(HEADS)] + [(4, h) for h in range(HEADS)]
        put(D_, "cond"), put(A_, "par", 1), put(B_, "par", 2), put(C_, "par", 3)
        put(C_, "ada", 0, 0)
        put_ab([("hT", 0, k) for k in range(DC)])
        put_ab([(n, j) for j in range(HC) for n in ("ga", "gb")])
        put_ab([(n, j) for n in ("q", "k") for j in range(HC)])
        for n in ("q", "k"):
            for j in range(HC):
                put((C_, D_)[j % 2], "rot", n, j)
        put_ab([("v", t) for t in range(NT)])
        put(C_, "kcT"), put(D_, "kout")
        put(A_, "ada", 0, 1), put(B_, "ada", 1, 0), put(A_, "ada", 1, 1)
        put(C_, "mean"), put(D_, "var")
        for u in range(len(UNITS)):
            put(A_, "s", u, 0), put(B_, "s", u, 1), put(C_, "aT", u), put(D_, "av", u)
        put_ab([("oT", h) for h in range(HEADS)])

        def put_tail(l):
            put_ab([("bc", l, q, c) for q in range(4) for c in range(2)])
            for i in range(2 * NT):
                put((C_, D_)[i % 2], "out", l, i)
            put_ab([("h2T", l, t) for t in range(NT)])
            put(C_, "logit", l)
            put(D_, "rank", l), put(D_, "table", l)

        put_tail(0)
        put_ab([("hT", 1, k) for k in range(DC)])
        for j in range(HC):
            put(A_, "hd", j), put(B_, "cg", j), put(C_, "bg", j), put(D_, "xc", j)
        put_ab([("pool", j) for j in range(HC)])
        put_tail(1)

        def fill(eng, *name):
            p, n = uses[name]
            if n:
                eng.wait_ge(psum_taken[p], n)
            return PB[p]

        def filled(ins, *name):
            ins.then_inc(psum_ready[uses[name][0]], 1)

        def take(eng, *name):
            p, n = uses[name]
            eng.wait_ge(psum_ready[p], n + 1)
            return PB[p]

        def took(ins, *name):
            ins.then_inc(psum_taken[uses[name][0]], 1)

        def after(eng, *name):
            p, n = uses[name]
            eng.wait_ge(psum_taken[p], n + 1)

        def chain(eng, name):
            s, n = sig(name), [0]

            def link(ins):
                ins.then_inc(s, 1)
                n[0] += 1
                eng.wait_ge(s, n[0])
            return link

        def cond_of(t):
            return 0 if t < 4 else 1

        block = ctx.enter_context(nc.Block())

        @block.sync
        def _(sp):
            sp.dma_start(X[:, 0:4, :], a["x_sample"][0].rearrange("(t p) d -> p t d", p=128)).then_inc(sig("x_loaded"), 16)
            sp.dma_start(X[:, 4, :], a["x_prompt"][0]).then_inc(sig("x_loaded"), 16)
            at = 0
            for l in range(2):
                while at < len(plan) and plan[at][0] == l:
                    _, name, src, s, used = plan[at]
                    if used:
                        sp.wait_ge(slot_free[s], used)
                    if l == 1 and page_at[name][1] - 1 == moe_base[0][0][s] + NE // 2:
                        sp.wait_ge(sig("down_done" if s == 2 else "gate_up_done", 0), 2 * NE if s == 3 else 2 * (NE - 1))
                    sp.dma_start(slot(s).rearrange("p (k n) -> p k n", k=DC), src).then_inc(slot_full[s], 16)
                    at += 1
                wg, wu = a["w_gate"][l], a["w_up"][l]
                wd = a["w_down"][l]

                def gate_page(w, e):
                    return w[bass.ds(e, 1)].rearrange("a (p k) n -> p (a k n)", k=DC)

                def down_page(e):
                    return wd[bass.ds(e, 1)].rearrange("a (j p) n -> (a p) j n", p=128)

                def expert(e, par, first):
                    for kind, w in enumerate((wg, wu, wd)):
                        s = 3 * par + kind
                        if first:
                            if s < 4:
                                sp.wait_ge(slot_free[s], moe_base[l][1][s])
                            elif s == 4:
                                sp.wait_ge(sig("mixer_out_done", l), 1)
                        elif kind != 1:
                            sp.wait_ge(sig("gate_up_done" if kind == 0 else "down_done", l), 2 * e - 2)
                        if kind < 2:
                            sp.dma_start(slot(s), gate_page(w, e)).then_inc(slot_full[s], 16)
                        else:
                            sp.dma_start(slot(s).rearrange("p (j n) -> p j n", j=HC), down_page(e)).then_inc(slot_full[s], 16)

                expert(0, 0, True)
                expert(1, 1, True)
                with nc.Fori(1, NE // 2, engines=(SP,)) as it:
                    for par in range(2):
                        expert(2 * it + par, par, False)
                sp.wait_ge(sig("routed", l), 1)
                nb = sp.value_load(NBK[0:1, 0:1], min_val=0, max_val=OVER)
                with nc.Fori(0, OVER, engines=(SP,)) as i:
                    with sp.If(nb > i):
                        e = sp.value_load(NBK[0:1, bass.ds(i + 1, 1)], min_val=0, max_val=NE - 1)
                        sp.wait_ge(sig("down_done", l), 2 * NE)
                        sp.dma_start(slot(0), gate_page(wg, e)).then_inc(sig("more_weights", l), 16)
                        sp.dma_start(slot(1), gate_page(wu, e)).then_inc(sig("more_weights", l), 16)
                        sp.dma_start(slot(2).rearrange("p (j n) -> p j n", j=HC), down_page(e)).then_inc(sig("more_weights", l), 16)
                        sp.wait_ge(sig("more_down", l), i + 1)
                        sp.sem_inc(sig("more_slots_back", l), 1)

        @block.gpsimd
        def _(pool):
            link = chain(pool, "pool_step")
            for k in (6, 7):
                after(pool, "hT", 0, k)
            for j in range(HC):
                for at in (0, 15 + NS, 30 + TOK):
                    ins = pool.memset(UP[:, j, at:at + 15], 0.0)
            link(ins)
            for j in range(HC):
                after(pool, "ga", j)
                after(pool, "gb", j)
                pool.tensor_tensor(UP[:, j, 15:15 + NS], GA[:, 0:NS], SG[:, 0:NS], ALU.mult)
                pool.tensor_tensor(UP[:, j, 30 + NS:30 + TOK], GA[:, NS:], SG[:, NS:], ALU.mult).then_inc(sig("u_ready"), 1)
            n = 0
            for name, dst in (("q", qT), ("k", kT)):
                for j in range(HC):
                    n += 1
                    after(pool, "rot", name, j)
                    pool.tensor_tensor(QC, dst[:, j, 0:NS], cos, ALU.mult)
                    link(pool.tensor_tensor(RQ, RQ, sin, ALU.mult))
                    pool.tensor_tensor(dst[:, j, 0:NS], QC, RQ, ALU.add).then_inc(sig("roped"), 1)

            for l in range(2):
                if l == 1:
                    pool.wait_ge(sig("combined", 0), 1)
                    for at in (0, 8 + NS, 16 + TOK):
                        pool.memset(XP[:, at:at + 8], 0.0)
                    for at in (0, 1 + NS, 2 + TOK):
                        ins = pool.memset(TP[:, at:at + 1], 0.0)
                    ins.then_inc(sig("pads_zero"), 1)
                pool.wait_ge(sig("mixer_out_done", l), 1)
                pool.wait_ge(sig("x_mixed", l), 2 * NT)
                pool.memset(XG[0], 0.0)
                link(pool.memset(XG[1], 0.0))
                pool.wait_ge(sig("routed", l), 1)
                pool.wait_ge(sig("h2_stored", l, 0), 16 * ((NT + 1) // 2))
                pool.wait_ge(sig("h2_stored", l, 1), 16 * (NT // 2))
                gathered = [sig("gathered", l, i) for i in range(2)]
                scattered = [sig("scattered", l, i) for i in range(2)]
                copied = sig("rows_copied", l)

                def gather(b, par, turns, steps):
                    pool.tensor_copy(GI[par][0:CAP, :], IDX[0:CAP, bass.ds(b, 1)]).then_inc(copied, 1)
                    pool.wait_ge(copied, steps)
                    if turns is not None:
                        pool.wait_ge(sig("x_turned", l), turns)
                    pool.sem_inc(sig("gather_issued", l), 1)
                    pool.indirect_dma_start(XG[par][0:CAP, :], None, h2_dram, bass.IndirectOffsetOnAxis(GI[par][0:CAP, :], 0),
                                            bounds_check=TOK - 1, oob_is_err=False).then_inc(gathered[par], 16)

                def scatter(b, par, before, steps):
                    if before is not None:
                        pool.wait_ge(scattered[par], before)
                    pool.sem_inc(sig("scatter_issued", l), 1)
                    pool.tensor_copy(SI[par][0:CAP, :], IDX[0:CAP, bass.ds(b + NBLK, 1)]).then_inc(copied, 1)
                    pool.wait_ge(copied, steps)
                    pool.wait_ge(sig("y_left", l), b + 1)
                    pool.wait_ge(sig("y_right", l), b + 1)
                    pool.sem_inc(sig("scatter_issued", l), 1)
                    pool.indirect_dma_start(y_dram, bass.IndirectOffsetOnAxis(SI[par][0:CAP, :], 0), YR[par][0:CAP, :], None,
                                            bounds_check=2 * TOK - 1, oob_is_err=False).then_inc(scattered[par], 16)

                gather(0, 0, None, 1)
                gather(1, 1, None, 2)
                scatter(0, 0, None, 3)
                gather(2, 0, 1, 4)
                scatter(1, 1, None, 5)
                with nc.Fori(1, NE // 2 - 1, engines=(POOL,)) as it:
                    for par in range(2):
                        b = 2 * it + par
                        gather(b + 1, 1 - par, b, 4 * it + 2 * par + 2)
                        scatter(b, par, 16 * it, 4 * it + 2 * par + 3)
                gather(NE - 1, 1, NE - 2, 2 * NE - 2)
                scatter(NE - 2, 0, 8 * NE - 16, 2 * NE - 1)
                scatter(NE - 1, 1, 8 * NE - 16, 2 * NE)
                for i in range(2):
                    pool.wait_ge(scattered[i], 8 * NE)
                nb = pool.value_load(NBK[0:1, 0:1], min_val=0, max_val=OVER)
                with nc.Fori(0, OVER, engines=(POOL,)) as i:
                    with pool.If(nb > i):
                        pool.tensor_copy(GI[0][0:CAP, :], IDX[0:CAP, bass.ds(i + NE, 1)])
                        pool.tensor_copy(SI[0][0:CAP, :], IDX[0:CAP, bass.ds(i + NE + NBLK, 1)]).then_inc(sig("more_copied", l), 1)
                        pool.wait_ge(sig("more_copied", l), i + 1)
                        pool.sem_inc(sig("gather_issued", l), 1)
                        pool.indirect_dma_start(XG[0][0:CAP, :], None, h2_dram, bass.IndirectOffsetOnAxis(GI[0][0:CAP, :], 0),
                                                bounds_check=TOK - 1, oob_is_err=False).then_inc(sig("more_gathered", l), 16)
                        pool.wait_ge(sig("more_left", l), i + 1)
                        pool.wait_ge(sig("more_right", l), i + 1)
                        pool.sem_inc(sig("scatter_issued", l), 1)
                        pool.indirect_dma_start(y_dram, bass.IndirectOffsetOnAxis(SI[0][0:CAP, :], 0), YR[0][0:CAP, :], None,
                                                bounds_check=2 * TOK - 1, oob_is_err=False).then_inc(sig("more_scattered", l), 16)
                        pool.wait_ge(sig("more_scattered", l), 16 * i + 16)
                        pool.sem_inc(sig("more_done", l), 1)
                pool.sem_inc(sig("experts_done", l), 1)

        @block.scalar
        def _(act):
            link = chain(act, "act_step")
            rows4, rows1, rows2, rows3 = (scr(14336 + 128 * i, 128) for i in range(4))
            act.dma_start(rows4[0:8, :], a["c"][0].rearrange("(k p) -> k p", p=128)).then_inc(sig("cond_loaded"), 16)
            act.dma_start(rows4[8:16, :], a["c_ctx"].rearrange("(k p) -> k p", p=128)).then_inc(sig("cond_loaded"), 16)
            act.dma_start(SQ[:, :], a["const_square"]).then_inc(sig("consts_loaded"), 16)
            n = 0
            for dst, parts in ((rows1, [a["b_ada"].rearrange("l (c p) -> (l c) p", p=128), a["g_norm1"].rearrange("l (c p) -> (l c) p", p=128),
                                        a["conv_a_b"].rearrange("l (c p) -> (l c) p", p=128), a["ln_a_g"].rearrange("l (c p) -> (l c) p", p=128),
                                        a["ln_a_b"].rearrange("l (c p) -> (l c) p", p=128), a["pool_scale"].rearrange("l (c p) -> (l c) p", p=128)]),
                               (rows2, [a["conv_a_w"][0].rearrange("t (c p) -> (t c) p", p=128), a["subln_g"]]),
                               (rows3, [a["conv_d_w"][0].rearrange("t (c p) -> (t c) p", p=128), a["g_norm2"].rearrange("l (c p) -> (l c) p", p=128)])):
                at = 0
                for src in parts:
                    m = src.shape[0]
                    act.dma_start(dst[at:at + m, :], src).then_inc(sig("params_loaded"), 16)
                    at += m
                    n += 1
            for i, nm in enumerate(("lam_q1", "lam_k1", "lam_q2", "lam_k2")):
                act.dma_start(LAMV[:, i * DH:(i + 1) * DH], a[nm][0].partition_broadcast(128)).then_inc(sig("lam_loaded"), 16)
            act.dma_start(IO[:, :], a["const_iotas"].partition_broadcast(128)).then_inc(sig("tables_loaded"), 16)
            act.dma_start(ROWS.rearrange("p s k t -> p (s k t)"), a["const_rows"]).then_inc(sig("tables_loaded"), 16)
            for l in range(2):
                act.dma_start(WR[:, l, :, 0:NG], a["w_router_g"][l].rearrange("(p k) g -> p k g", k=DC)).then_inc(sig("tables_loaded"), 16)
                for g in range(NG):
                    act.dma_start(WR[:, l, :, NG + g * EPG:NG + (g + 1) * EPG],
                                  a["w_router_e"][l, g].rearrange("(p k) e -> p k e", k=DC)).then_inc(sig("tables_loaded"), 16)
                act.dma_start(BR[:, l, 0:NG], a["b_router_g"][l].partition_broadcast(128)).then_inc(sig("tables_loaded"), 16)
                act.dma_start(BR[:, l, NG:36], a["b_router_e"][l].rearrange("g e -> (g e)").partition_broadcast(128)).then_inc(sig("tables_loaded"), 16)
            act.dma_start(KC, a["cache_k"].rearrange("b l t h c d -> (b l t) (h c d)")).then_inc(sig("cache_loaded"), 16)
            act.dma_start(VC, a["cache_v"].rearrange("b l t h c -> (b l t) (h c)")).then_inc(sig("cache_loaded"), 16)

            act.wait_ge(sig("cond_loaded"), 32)
            act.activation(rows4[0:16, :], rows4[0:16, :], ACT.Silu).then_inc(sig("cond_ready"), 1)
            act.wait_ge(sig("lam_dots"), 1)
            act.activation(laml, lam2, ACT.Exp).then_inc(sig("lam_exps"), 1)

            def squares(gate, junk):
                for t in range(NT):
                    gate(t)
                    act.activation(junk, X[:, t, :], ACT.Square, accum_out=ssq[:, t:t + 1]).then_inc(sig("squares_done"), 1)
                    act.wait_ge(sig("squares_done"), NT * NORM[0] + t + 1)
                NORM[0] += 1
                act.wait_ge(sig("mean_square"), NORM[0])
                act.activation(rstd, rstd, ACT.Sqrt).then_inc(sig("root_done"), 1)

            NORM = [0]

            def first_norm(l):
                def gate(t):
                    if l == 0:
                        act.wait_ge(sig("x_loaded"), 32)
                    else:
                        act.wait_ge(sig("combined", 0), t + 1)
                squares(gate, junk1)
                for k in range(0, DC, 2):
                    p = take(act, "hT", l, k)
                    if k == 0:
                        act.wait_ge(sig("modulated", l), 1)
                    act.activation(hT[:, k, 0:NS], p[:, 0:NS], ACT.Identity, bias=MOD[:, l, k, 0:1], scale=SC1[:, l, k, 0:1])
                    took(act.activation(hT[:, k, NS:], p[:, NS:TOK], ACT.Identity, bias=MOD[:, l, k, 1:2], scale=SC1[:, l, k, 1:2]), "hT", l, k)

            def tail(l):
                for q in range(4):
                    for c in range(2):
                        p = take(act, "bc", l, q, c)
                        dst = (BC[:, 0, c], BC[:, 1, c], M2[:, 0, c], M2[:, 1, c])[q]
                        took(act.activation(dst, p[:, :], ACT.Copy), "bc", l, q, c)
                squares(lambda t: act.wait_ge(sig("x_mixed", l), NT + t + 1), junk2)
                for t in range(NT):
                    act.wait_ge(sig("h2_ready", l), t + 1)
                    act.dma_start(h2_dram[t * 128:(t + 1) * 128, :], H2[t % 2]).then_inc(sig("h2_stored", l, t % 2), 16)
                    p = take(act, "h2T", l, t)
                    if t >= 2:
                        act.wait_ge(sig("tile_routed", l), t - 1)
                    took(act.activation(H2T[t % 2].rearrange("p k t -> p (k t)"), p[:, :], ACT.Copy), "h2T", l, t)
                act.wait_ge(sig("router_z", l), 1)
                act.activation(scr(RT + 0, 20), scr(RT + 0, 20), ACT.Exp).then_inc(sig("router_exp", l), 1)
                act.wait_ge(sig("router_z", l), 2)
                act.activation(scr(RT + 20, 5), scr(RT + 20, 5), ACT.Exp).then_inc(sig("router_exp", l), 1)

            def experts(l):
                xt, gu, hid, yd = (sig(n, l) for n in ("x_turned", "gate_up_done", "hidden", "down_done"))

                def turn(b1, par):
                    act.wait_ge(xt, b1)
                    act.activation(XGT[par].rearrange("p (b c) -> p b c", b=2), PB[A_][:, :].rearrange("p (b c) -> p b c", b=2)[:, :, 0:4 * CAP],
                                   ACT.Copy).then_inc(sig("x_ready", l), 1)

                def body(b, par, first, last, before):
                    for h in range(2):
                        act.wait_ge(gu, 2 * b + h + 1)
                        act.activation(SIL[:, 2 * CAP * h:2 * CAP * (h + 1)], PB[B_][:, 512 * h:512 * h + 2 * CAP],
                                       ACT.Silu).then_inc(sig("silu", l), 1)
                    if not last:
                        turn(b + 2, 1 - par)
                    act.wait_ge(yd, 2 * b + 1)
                    if before is not None:
                        act.wait_ge(sig("scattered", l, par), before)
                    act.activation(YR[par][0:CAP, 0:512], PB[C_][0:CAP, 0:512], ACT.Copy).then_inc(sig("y_left", l), 1)

                turn(1, 0)
                body(0, 0, True, False, None)
                body(1, 1, False, False, None)
                with nc.Fori(1, NE // 2 - 1, engines=(ACTE,)) as it:
                    for par in range(2):
                        body(2 * it + par, par, False, False, 16 * it)
                body(NE - 2, 0, False, False, 8 * NE - 16)
                body(NE - 1, 1, False, True, 8 * NE - 16)
                for i in range(2):
                    act.wait_ge(sig("scattered", l, i), 8 * NE)
                nb = act.value_load(NBK[0:1, 0:1], min_val=0, max_val=OVER)
                with nc.Fori(0, OVER, engines=(ACTE,)) as i:
                    with act.If(nb > i):
                        act.wait_ge(sig("more_turned", l), i + 1)
                        act.activation(XGT[0].rearrange("p (b c) -> p b c", b=2), PB[A_][:, :].rearrange("p (b c) -> p b c", b=2)[:, :, 0:4 * CAP],
                                       ACT.Copy).then_inc(sig("more_x_ready", l), 1)
                        act.wait_ge(sig("more_gate_up", l), i + 1)
                        act.activation(SIL.rearrange("p (h c) -> p h c", h=2), HALVES[:, :, 0:2 * CAP], ACT.Silu).then_inc(sig("more_silu", l), 1)
                        act.wait_ge(sig("more_down", l), i + 1)
                        act.activation(YR[0][0:CAP, 0:512], PB[C_][0:CAP, 0:512], ACT.Copy).then_inc(sig("more_left", l), 1)
                act.wait_ge(sig("experts_done", l), 1)
                rows = y_dram.rearrange("(t p two) d -> t p (two d)", p=128, two=2)
                for t in range(NT):
                    if t >= 2:
                        act.wait_ge(sig("combined", l), t - 1)
                    act.dma_start(YB[t % 2], rows[t]).then_inc(sig("y_back", l, t % 2), 16)

            first_norm(0)
            for j in range(HC):
                p = take(act, "ga", j)
                if j:
                    act.wait_ge(sig("u_ready"), j)
                took(act.activation(GA, p[:, 0:TOK], ACT.Copy), "ga", j)
                p = take(act, "gb", j)
                took(act.activation(SG, p[:, 0:TOK], ACT.Sigmoid), "gb", j)
            for name, dst in (("q", qT), ("k", kT)):
                for j in range(HC):
                    p = take(act, name, j)
                    took(act.activation(dst[:, j, :], p[:, 0:TOK], ACT.Copy), name, j)
            n = 0
            for name in ("q", "k"):
                for j in range(HC):
                    p = take(act, "rot", name, j)
                    if n:
                        act.wait_ge(sig("roped"), n)
                    n += 1
                    took(act.activation(RQ, p[:, 0:NS], ACT.Copy), "rot", name, j)
            for t in range(NT):
                p = take(act, "v", t)
                took(act.activation(V[:, t, :], p[:, 0:HALF], ACT.Copy), "v", t)
            p = take(act, "kcT")
            took(act.activation(kcT.rearrange("p h t -> p (h t)"), p[:, 0:HALF], ACT.Copy), "kcT")
            p = take(act, "kout")
            took(act.activation(KC, p[:, 0:HALF], ACT.Copy), "kout")
            after(act, "kout")
            act.dma_start(out["new_cache_k"].rearrange("b l t h c d -> (b l t) (h c d)"), KC).then_inc(sig("outputs_stored"), 16)
            after(act, "v", 4)
            act.dma_start(out["new_cache_v"].rearrange("b l t h c -> (b l t) (h c)"), V[:, 4, :]).then_inc(sig("outputs_stored"), 16)
            p = take(act, "mean")
            took(act.activation(MU[:, 0:TOK], p[:, 0:TOK], ACT.Copy, scale=1.0 / HALF), "mean")
            for j in range(HC):
                act.wait_ge(sig("centred"), j + 1)
                if j >= 2:
                    act.wait_ge(sig("squares_summed"), j - 1)
                act.activation(SQB[j % 2], UO[:, j, :], ACT.Square).then_inc(sig("conv_squares"), 1)
            p = take(act, "var")
            act.wait_ge(sig("eps_ready"), 1)
            act.wait_ge(sig("roped"), 8)
            took(act.activation(RS[:, 0:TOK], p[:, 0:TOK], ACT.Sqrt, bias=eps1, scale=1.0 / HALF), "var")
            for j in range(HC):
                act.wait_ge(sig("conv_normed"), j + 1)
                act.activation(catU[:, j, 0:NS], UO[:, j, 0:NS], ACT.Silu, bias=ln_bT[:, j:j + 1], scale=ln_gT[:, j:j + 1])
                act.activation(catU[:, j, NS:], UO[:, j, 15 + NS:], ACT.Silu, bias=ln_bT[:, j:j + 1], scale=ln_gT[:, j:j + 1]).then_inc(sig("cat_u"), 1)

            def exps(u):
                w = NS + PAST if UNITS[u][0] < 4 else NP
                for c in range(2):
                    take(act, "s", u, c)
                    act.wait_ge(sig("max_ready"), 2 * u + c + 1)
                    if u >= 2 and c == 0:
                        take(act, "aT", u - 2)
                    took(act.activation(PR[:, u % 2, c, 0:w], PB[uses[("s", u, c)][0]][:, 0:w], ACT.Exp, bias=snb[:, u % 2, c:c + 1],
                                        scale=DH ** -0.5, accum_out=sl[:, u % 2, c:c + 1]), "s", u, c)

            def turned(u):
                w = NS + PAST if UNITS[u][0] < 4 else NP
                p = take(act, "aT", u)
                if u >= 2:
                    take(act, "av", u - 2)
                took(act.activation(AT[:, u % 2, 0:w], p[:, 0:w], ACT.Copy), "aT", u)

            NU = len(UNITS)
            for i in range(NU + 1):
                if i < NU:
                    exps(i)
                if i >= 1:
                    turned(i - 1)
            act.wait_ge(sig("o_mean_square"), 1)
            act.activation(orstd, orstd, ACT.Sqrt).then_inc(sig("o_root"), 1)
            act.wait_ge(sig("subln_ready"), 1)
            for h in range(HEADS):
                p = take(act, "oT", h)
                took(act.activation(oT[:, h, :], p[:, 0:TOK], ACT.Copy, scale=sub2), "oT", h)
            tail(0)
            experts(0)

            act.wait_ge(sig("combined", 0), NT)
            act.dma_start(CNT.rearrange("p j t -> p (j t)"), a["const_counts"].partition_broadcast(128)).then_inc(sig("counts_loaded"), 16)
            act.dma_start(PW, a["pool_w"][0].rearrange("g c e -> c g e")).then_inc(sig("counts_loaded"), 16)
            first_norm(1)
            for j in range(HC):
                p = take(act, "hd", j)
                if j:
                    act.wait_ge(sig("gated_in"), j)
                took(act.activation(HD, p[:, 0:TOK], ACT.Copy), "hd", j)
                p = take(act, "cg", j)
                took(act.activation(CG, p[:, 0:TOK], ACT.Copy), "cg", j)
                p = take(act, "bg", j)
                if j:
                    act.wait_ge(sig("short_conv"), j)
                took(act.activation(BG, p[:, 0:TOK], ACT.Copy), "bg", j)
                p = take(act, "xc", j)
                if j:
                    act.wait_ge(sig("pooled"), j)
                else:
                    act.wait_ge(sig("pads_zero"), 1)
                act.activation(XP[:, 8:8 + NS], p[:, 0:NS], ACT.Copy)
                took(act.activation(XP[:, 16 + NS:16 + TOK], p[:, NS:TOK], ACT.Copy), "xc", j)
            for j in range(HC):
                p = take(act, "pool", j)
                took(act.activation(CAT[:, j, :], p[:, 0:TOK], ACT.Copy, scale=pool_sT[:, j:j + 1]), "pool", j)
            tail(1)
            experts(1)
            act.wait_ge(sig("combined", 1), NT)
            act.dma_start(GF, a["g_final"].partition_broadcast(128)).then_inc(sig("final_gain"), 16)
            squares(lambda t: None, junk1)
            for t in range(NT):
                act.wait_ge(sig("y_final"), t + 1)
                dst = out["y_sample"][0, 128 * t:128 * (t + 1), :] if t < 4 else out["y_prompt"][0]
                act.dma_start(dst, X[:, t, :]).then_inc(sig("outputs_stored"), 16)
            act.wait_ge(sig("outputs_stored"), 16 * (2 + NT))

        @block.vector
        def _(dve):
            link = chain(dve, "vector_step")
            tt, ts, stt = dve.tensor_tensor, dve.tensor_scalar, dve.scalar_tensor_tensor
            dve.memset(eps1, EPS).then_inc(sig("eps_ready"), 1)
            dve.wait_ge(sig("lam_loaded"), 64)
            lv = LAMV.rearrange("p (i two d) -> p i two d", i=2, two=2)
            link(tt(lv[:, :, 0, :], lv[:, :, 0, :], lv[:, :, 1, :], ALU.mult))
            dve.tensor_reduce(lam2, lv[:, :, 0, :], AX_X, ALU.add).then_inc(sig("lam_dots"), 1)
            dve.wait_ge(sig("lam_exps"), 1)
            link(tt(lam_neg, laml[:, 1:2], laml[:, 0:1], ALU.subtract))
            link(ts(lam_neg, lam_neg, -LAM_INIT, None, ALU.add))
            p = take(dve, "cond")
            took(dve.tensor_copy(condT[:, :], p[:, 0:16]), "cond")
            for i, (dst, w) in enumerate(((P1, 128), (P2, 125), (P3, 28))):
                p = take(dve, "par", i + 1)
                took(dve.tensor_copy(dst[:, :], p[:, 0:w]), "par", i + 1)
            for i in (1, 2, 3):
                after(dve, "par", i)
            ts(sub2, sublnT, 1.0 - LAM_INIT, None, ALU.mult).then_inc(sig("subln_ready"), 1)

            def modulation(l, part):
                p = take(dve, "ada", l, part)
                lo, hi = (0, 16) if part == 0 else (16, 48)
                took(tt(MOD[:, l, lo:hi, :], p[:, 2 * lo:2 * hi].rearrange("p (c s) -> p c s", s=2),
                        b_adaT[:, l, lo:hi].unsqueeze(2).broadcast_to([128, hi - lo, 2]), ALU.add), "ada", l, part)
                after(dve, "ada", l, part)
                if part == 0:
                    ins = stt(SC1[:, l], MOD[:, l, 8:16, :], 1.0, g_n1T[:, l, :].unsqueeze(2).broadcast_to([128, DC, 2]), ALU.add, ALU.mult)
                    ins.then_inc(sig("modulated", l), 1)
                else:
                    ins = stt(SC2[:, l], MOD[:, l, 32:40, :], 1.0, g_n2T[:, l, :].unsqueeze(2).broadcast_to([128, DC, 2]), ALU.add, ALU.mult)
                    ins.then_inc(sig("modulated2", l), 1)

            NORM = [0]

            def inverse_root():
                NORM[0] += 1
                dve.wait_ge(sig("squares_done"), NT * NORM[0])
                ts(rstd, ssq, 1.0 / D, EPS, ALU.mult, ALU.add).then_inc(sig("mean_square"), 1)
                dve.wait_ge(sig("root_done"), NORM[0])
                link(dve.reciprocal(rstd, rstd))

            def first_norm(l):
                inverse_root()
                for t in range(NT):
                    ts(XN[:, t, :], X[:, t, :], rstd[:, t:t + 1], None, ALU.mult).then_inc(sig("normed", l), 1)
                for k in range(1, DC, 2):
                    if k == 1:
                        dve.wait_ge(sig("modulated", l), 1)
                    p = take(dve, "hT", l, k)
                    ts(hT[:, k, 0:NS], p[:, 0:NS], SC1[:, l, k, 0:1], MOD[:, l, k, 0:1], ALU.mult, ALU.add)
                    took(ts(hT[:, k, NS:], p[:, NS:TOK], SC1[:, l, k, 1:2], MOD[:, l, k, 1:2], ALU.mult, ALU.add), "hT", l, k)

            def residual(l):
                for i in range(2 * NT):
                    n, t = divmod(i, NT)
                    if i == 0:
                        for c in range(2):
                            after(dve, "bc", l, 0, c)
                    p = take(dve, "out", l, i)
                    cols = slice(n * 512, (n + 1) * 512)
                    took(tt(TMP[0], p[:, 0:512], BC[:, 0, cond_of(t), cols], ALU.mult), "out", l, i)
                    after(dve, "out", l, i)
                    tt(X[:, t, cols], X[:, t, cols], TMP[0], ALU.add).then_inc(sig("x_mixed", l), 1)
                    dve.wait_ge(sig("x_mixed", l), i + 1)

            def second_norm(l):
                inverse_root()
                for q in (2, 3):
                    for c in range(2):
                        after(dve, "bc", l, q, c)
                for t in range(NT):
                    if t >= 2:
                        take(dve, "h2T", l, t - 2)
                        dve.wait_ge(sig("h2_stored", l, t % 2), 16 * (t // 2))
                    link(stt(H2[t % 2], X[:, t, :], rstd[:, t:t + 1], M2[:, 0, cond_of(t)], ALU.mult, ALU.mult))
                    tt(H2[t % 2], H2[t % 2], M2[:, 1, cond_of(t)], ALU.add).then_inc(sig("h2_ready", l), 1)

            def routing(l):
                at = [BOTH_AT + NT * NE]
                dve.wait_ge(sig("tables_loaded"), 16 * 16)

                def tmp(*shape):
                    n = int(np.prod(shape))
                    v = scr(at[0], n)
                    at[0] += n
                    if len(shape) == 2:
                        v = v.rearrange("p (a b) -> p a b", a=shape[0])
                    if len(shape) == 3:
                        v = v.rearrange("p (a b c) -> p a b c", a=shape[0], b=shape[1])
                    return v

                LG = tmp(NT, 36)
                p = take(dve, "logit", l)
                took(tt(LG, p[:, 0:36 * NT].rearrange("p (t n) -> p t n", t=NT), BR[:, l, :].unsqueeze(1).broadcast_to([128, NT, 36]), ALU.add), "logit", l)
                after(dve, "logit", l)
                gl = LG[:, :, 0:NG]
                el = LG[:, :, NG:].rearrange("p t (g e) -> p t g e", g=NG)
                top = lambda v, n: v.unsqueeze(2).broadcast_to([128, NT, n])
                gm, gi = tmp(NT), tmp(NT)
                oh = tmp(NT, NG)
                z = scr(RT, 20).rearrange("p (t g) -> p t g", g=NG)
                iog = iota["g"].unsqueeze(1).broadcast_to([128, NT, NG])
                ioe = iota["e"].unsqueeze(1).broadcast_to([128, NT, EPG])
                link(dve.tensor_reduce(gm, gl, AX_X, ALU.max))
                tt(z, gl, top(gm, NG), ALU.subtract).then_inc(sig("router_z", l), 1)
                link(tt(oh, gl, top(gm, NG), ALU.is_equal))
                link(tt(oh, oh, iog, ALU.mult))
                link(dve.tensor_reduce(gi, oh, AX_X, ALU.min))
                link(tt(oh, iog, top(gi, NG), ALU.is_equal))
                prod, e8 = tmp(NT * NG, EPG), tmp(NT, EPG)
                pv = prod.rearrange("p (t g) e -> p t g e", g=NG)
                link(tt(pv, el, oh.unsqueeze(3).broadcast_to([128, NT, NG, EPG]), ALU.mult))
                link(dve.tensor_reduce(e8, pv.rearrange("p t g e -> p t e g"), AX_X, ALU.add))
                ohe = tmp(2, NT * EPG).rearrange("p k (t e) -> p k t e", t=NT)
                vm, vi = tmp(2, NT), tmp(NT)
                for k in range(2):
                    link(dve.tensor_reduce(vm[:, k], e8, AX_X, ALU.max))
                    link(tt(ohe[:, k], e8, top(vm[:, k], EPG), ALU.is_equal))
                    link(tt(ohe[:, k], ohe[:, k], ioe, ALU.mult))
                    link(dve.tensor_reduce(vi, ohe[:, k], AX_X, ALU.min))
                    link(tt(ohe[:, k], ioe, top(vi, EPG), ALU.is_equal))
                    if k == 0:
                        link(stt(e8, ohe[:, 0], -3e38, e8, ALU.mult, ALU.add))
                e2 = scr(RT + 20, 5)
                tt(e2, vm[:, 1], vm[:, 0], ALU.subtract).then_inc(sig("router_z", l), 1)
                ch = tmp(2, NT * NE)
                ch5 = ch.rearrange("p k (t g e) -> p k t g e", t=NT, g=NG)
                for k in range(2):
                    for t in range(NT):
                        ins = tt(ch5[:, k, t], oh[:, t, :].unsqueeze(2).broadcast_to([128, NG, EPG]),
                                 ohe[:, k, t, :].unsqueeze(1).broadcast_to([128, NG, EPG]), ALU.mult)
                link(ins)
                both = scr(BOTH_AT, NT * NE)
                tt(both, ch[:, 0], ch[:, 1], ALU.add).then_inc(sig("chosen", l), 1)
                dve.wait_ge(sig("router_exp", l), 1)
                gs = tmp(NT)
                link(dve.tensor_reduce(gs, z, AX_X, ALU.add))
                dve.wait_ge(sig("router_exp", l), 2)
                d2 = tmp(NT)
                link(ts(d2, e2, 1.0, None, ALU.add))
                link(tt(gs, gs, d2, ALU.mult))
                link(dve.reciprocal(WT1, gs))
                link(tt(WT2, WT1, e2, ALU.mult))
                p = take(dve, "rank", l)
                rk = tmp(192)
                took(dve.tensor_copy(rk, p[:, 0:192]), "rank", l)
                after(dve, "rank", l)
                ranks, cnt = rk[:, 0:160], rk[:, 160:192]
                nov, ovs, ovt = tmp(NE), tmp(NE), tmp(NE)
                link(ts(nov, cnt, float(CAP), None, ALU.is_gt))
                for j in range(2, MORE + 1):
                    link(stt(nov, cnt, float(CAP * j), nov, ALU.is_gt, ALU.add))
                src, dst = nov, ovs
                for s in (1, 2, 4, 8, 16):
                    tt(dst[:, s:], src[:, s:], src[:, :NE - s], ALU.add)
                    link(dve.tensor_copy(dst[:, 0:s], src[:, 0:s]))
                    src, dst = dst, (ovt if dst is ovs else ovs)
                ove = src
                start = dst
                link(tt(start, ove, nov, ALU.subtract))
                cmp = prod.rearrange("p a b -> p (a b)")
                ebk = tmp(OVER)
                for half in ((0, 5), (5, 10), (10, OVER)):
                    m = half[1] - half[0]
                    c3 = cmp[:, 0:m * NE].rearrange("p (a b) -> p a b", a=m)
                    link(tt(c3, ove.unsqueeze(1).broadcast_to([128, m, NE]),
                            iota["o"][:, half[0]:half[1]].unsqueeze(2).broadcast_to([128, m, NE]), ALU.is_le))
                    link(dve.tensor_reduce(ebk[:, half[0]:half[1]], c3, AX_X, ALU.add))
                link(ts(ebk, ebk, float(NE - 1), None, ALU.min))
                dve.tensor_copy(NBK[:, 0:1], ove[:, NE - 1:NE])
                link(dve.tensor_copy(NBK[:, 1:], ebk))
                res = tmp(3, 2 * NT)
                for w in range(3):
                    for k in range(2):
                        c3 = cmp[:, 0:NT * NE].rearrange("p (t e) -> p t e", t=NT)
                        m1 = ch[:, k].rearrange("p (t e) -> p t e", t=NT)
                        m2 = (ranks.rearrange("p (t e) -> p t e", t=NT), iota["E"].unsqueeze(1).broadcast_to([128, NT, NE]),
                              start.unsqueeze(1).broadcast_to([128, NT, NE]))[w]
                        link(tt(c3, m1, m2, ALU.mult))
                        link(dve.tensor_reduce(res[:, w, k * NT:(k + 1) * NT], c3, AX_X, ALU.add))
                rank, exp_, st_ = res[:, 0], res[:, 1], res[:, 2]
                q, gt = tmp(10), tmp(10)
                link(ts(q, rank, float(CAP), None, ALU.is_ge))
                link(ts(gt, q, 1.0, None, ALU.mult))
                for j in range(2, MORE + 1):
                    link(stt(q, rank, float(CAP * j), q, ALU.is_ge, ALU.add))
                link(stt(rank, q, -float(CAP), rank, ALU.mult, ALU.add))
                link(tt(st_, st_, q, ALU.add))
                link(ts(st_, st_, float(NE - 1), None, ALU.add))
                link(tt(st_, st_, exp_, ALU.subtract))
                link(tt(st_, st_, gt, ALU.mult))
                link(tt(exp_, exp_, st_, ALU.add))
                for i in range(10):
                    k, t = divmod(i, NT)
                    ts(POSH[:, i, :], iota["c"], rank[:, i:i + 1], None, ALU.is_equal)
                    for s in range(2):
                        ins = ts(VAL[:, i, s, :], iota["b"], exp_[:, i:i + 1], ROWS[:, s, k, t:t + 1], ALU.is_equal, ALU.mult)
                ins.then_inc(sig("one_hots", l), 1)
                p = take(dve, "table", l)
                took(ts(IDX[0:CAP, :], p[0:CAP, 0:2 * NBLK], NOROW, None, ALU.add), "table", l)
                after(dve, "table", l)
                dve.memset(small[:, 157:158], 0.0).then_inc(sig("routed", l), 1)

            def experts(l):
                def body(b, par, before):
                    for h in range(2):
                        dve.wait_ge(sig("silu", l), 2 * b + h + 1)
                        cols = slice(2 * CAP * h, 2 * CAP * (h + 1))
                        tt(HIDT[par][:, cols], PB[B_][:, 512 * h + 2 * CAP:512 * h + 4 * CAP], SIL[:, cols], ALU.mult).then_inc(sig("hidden", l), 1)
                    dve.wait_ge(sig("down_done", l), 2 * b + 2)
                    if before is not None:
                        dve.wait_ge(sig("scattered", l, par), before)
                    dve.tensor_copy(YR[par][0:CAP, 512:1024], PB[C_][0:CAP, 512:1024]).then_inc(sig("y_right", l), 1)

                body(0, 0, None)
                body(1, 1, None)
                with nc.Fori(1, NE // 2, engines=(DVE,)) as it:
                    for par in range(2):
                        body(2 * it + par, par, 16 * it)
                for i in range(2):
                    dve.wait_ge(sig("scattered", l, i), 8 * NE)
                nb = dve.value_load(NBK[0:1, 0:1], min_val=0, max_val=OVER)
                with nc.Fori(0, OVER, engines=(DVE,)) as i:
                    with dve.If(nb > i):
                        dve.wait_ge(sig("more_silu", l), i + 1)
                        tt(HIDT[0].rearrange("p (h c) -> p h c", h=2), HALVES[:, :, 2 * CAP:4 * CAP], SIL.rearrange("p (h c) -> p h c", h=2),
                           ALU.mult).then_inc(sig("more_hidden", l), 1)
                        dve.wait_ge(sig("more_down", l), i + 1)
                        dve.tensor_copy(YR[0][0:CAP, 512:1024], PB[C_][0:CAP, 512:1024]).then_inc(sig("more_right", l), 1)
                for t in range(NT):
                    dve.wait_ge(sig("y_back", l, t % 2), 16 * (t // 2 + 1))
                    y = YB[t % 2]
                    link(ts(y[:, 0:D], y[:, 0:D], WT1[:, t:t + 1], None, ALU.mult))
                    link(stt(y[:, 0:D], y[:, D:], WT2[:, t:t + 1], y[:, 0:D], ALU.mult, ALU.add))
                    link(tt(y[:, 0:D], y[:, 0:D], BC[:, 1, cond_of(t)], ALU.mult))
                    tt(X[:, t, :], X[:, t, :], y[:, 0:D], ALU.add).then_inc(sig("combined", l), 1)
                dve.wait_ge(sig("combined", l), NT)

            modulation(0, 0)
            dve.wait_ge(sig("x_loaded"), 32)
            first_norm(0)
            for j0 in (0, 2):
                for tap in range(TAPS):
                    for j in (j0, j0 + 1):
                        if tap == 0:
                            dve.wait_ge(sig("u_ready"), j + 1)
                            ts(UO[:, j, :], UP[:, j, 0:UOW], conv_wT[:, 0, j:j + 1], conv_bT[:, j:j + 1], ALU.mult, ALU.add).then_inc(sig("conv_step", j), 1)
                        else:
                            dve.wait_ge(sig("conv_step", j), tap)
                            stt(UO[:, j, :], UP[:, j, tap:tap + UOW], conv_wT[:, tap, j:j + 1], UO[:, j, :], ALU.mult, ALU.add).then_inc(sig("conv_step", j), 1)
            modulation(0, 1)
            modulation(1, 0)
            modulation(1, 1)
            after(dve, "mean")
            for j in range(HC):
                dve.wait_ge(sig("conv_step", j), TAPS)
                tt(UO[:, j, 0:NS], UO[:, j, 0:NS], MU[:, 0:NS], ALU.subtract)
                tt(UO[:, j, 15 + NS:], UO[:, j, 15 + NS:], MU[:, NS:TOK], ALU.subtract).then_inc(sig("centred"), 1)
            after(dve, "var")
            link(dve.reciprocal(RS[:, 0:TOK], RS[:, 0:TOK]))
            dve.wait_ge(sig("centred"), HC)
            dve.wait_ge(sig("conv_squares"), HC)
            for j in range(HC):
                tt(UO[:, j, 0:NS], UO[:, j, 0:NS], RS[:, 0:NS], ALU.mult)
                tt(UO[:, j, 15 + NS:], UO[:, j, 15 + NS:], RS[:, NS:TOK], ALU.mult).then_inc(sig("conv_normed"), 1)

            def maxima(u):
                w = NS + PAST if UNITS[u][0] < 4 else NP
                for c in range(2):
                    p = take(dve, "s", u, c)
                    link(dve.tensor_reduce(smx[:, u % 2, c:c + 1], p[:, 0:w], AX_X, ALU.max))
                    ts(snb[:, u % 2, c:c + 1], smx[:, u % 2, c:c + 1], -DH ** -0.5, None, ALU.mult).then_inc(sig("max_ready"), 1)

            def mixed(u):
                w = NS + PAST if UNITS[u][0] < 4 else NP
                for c in range(2):
                    after(dve, "s", u, c)
                link(dve.reciprocal(sr[:, u % 2, :], sl[:, u % 2, :]))
                link(tt(sr[:, u % 2, 1:2], sr[:, u % 2, 1:2], lam_neg, ALU.mult))
                link(ts(PR[:, u % 2, 1, 0:w], PR[:, u % 2, 1, 0:w], sr[:, u % 2, 1:2], None, ALU.mult))
                stt(PR[:, u % 2, 0, 0:w], PR[:, u % 2, 0, 0:w], sr[:, u % 2, 0:1], PR[:, u % 2, 1, 0:w], ALU.mult, ALU.add).then_inc(sig("a_ready"), 1)

            def heads_out(u):
                t, h = UNITS[u]
                p = take(dve, "av", u)
                took(dve.tensor_copy(OR[:, t, h * 128:(h + 1) * 128], p[:, 0:128]), "av", u)

            NU = len(UNITS)
            for i in range(NU + 2):
                if i < NU:
                    maxima(i)
                if 1 <= i <= NU:
                    mixed(i - 1)
                if i >= 2:
                    heads_out(i - 2)
            after(dve, "av", NU - 1)
            sq = PR.rearrange("p u c t -> p (u c t)")
            flat = OR.rearrange("p t n -> p (t n)")
            link(tt(sq, flat, flat, ALU.mult))
            link(dve.tensor_reduce(oss, sq.rearrange("p (u e) -> p u e", e=128), AX_X, ALU.add))
            ts(orstd, oss, 1.0 / 128, EPS, ALU.mult, ALU.add).then_inc(sig("o_mean_square"), 1)
            dve.wait_ge(sig("o_root"), 1)
            link(dve.reciprocal(orstd, orstd))
            o3 = flat.rearrange("p (u e) -> p u e", e=128)
            tt(o3, o3, orstd.unsqueeze(2).broadcast_to([128, 20, 128]), ALU.mult).then_inc(sig("o_normed"), 1)
            residual(0)
            second_norm(0)
            routing(0)
            experts(0)

            first_norm(1)
            dve.wait_ge(sig("counts_loaded"), 32)
            dve.wait_ge(sig("pads_zero"), 1)
            for j in range(HC):
                after(dve, "cg", j)
                after(dve, "hd", j)
                tt(TP[:, 1:1 + NS], HD[:, 0:NS], CG[:, 0:NS], ALU.mult)
                tt(TP[:, 2 + NS:2 + TOK], HD[:, NS:], CG[:, NS:], ALU.mult).then_inc(sig("gated_in"), 1)
                dve.wait_ge(sig("gated_in"), j + 1)
                W3 = TOK + 1
                link(ts(CA[:, 0:W3], TP[:, 0:W3], sconv_wT[:, 0, j:j + 1], None, ALU.mult))
                link(stt(CA[:, 0:W3], TP[:, 1:1 + W3], sconv_wT[:, 1, j:j + 1], CA[:, 0:W3], ALU.mult, ALU.add))
                link(stt(CA[:, 0:W3], TP[:, 2:2 + W3], sconv_wT[:, 2, j:j + 1], CA[:, 0:W3], ALU.mult, ALU.add))
                after(dve, "bg", j)
                tt(CAT[:, 4 + j, 0:NS], CA[:, 0:NS], BG[:, 0:NS], ALU.mult)
                tt(CAT[:, 4 + j, NS:], CA[:, 1 + NS:1 + TOK], BG[:, NS:], ALU.mult).then_inc(sig("short_conv"), 1)
                after(dve, "xc", j)
                src, n = XP, XPW
                for s in range(j + 1):
                    n -= 1 << s
                    dst = PS2[s % 2]
                    link(tt(dst[:, 0:n], src[:, 0:n], src[:, 1 << s:(1 << s) + n], ALU.add))
                    src = dst
                half = WINDOWS[j] // 2
                tt(DP[:, j, 0:NS], src[:, 8 - half:8 - half + NS], CNT[:, j, 0:NS], ALU.mult)
                link(tt(DP[:, j, NS:], src[:, 16 + NS - half:16 + TOK - half], CNT[:, j, NS:], ALU.mult))
                tt(DP[:, j, 0:NS], DP[:, j, 0:NS], XP[:, 8:8 + NS], ALU.subtract)
                tt(DP[:, j, NS:], DP[:, j, NS:], XP[:, 16 + NS:16 + TOK], ALU.subtract).then_inc(sig("pooled"), 1)
            residual(1)
            second_norm(1)
            routing(1)
            experts(1)
            inverse_root()
            dve.wait_ge(sig("final_gain"), 16)
            for t in range(NT):
                stt(X[:, t, :], X[:, t, :], rstd[:, t:t + 1], GF, ALU.mult, ALU.mult).then_inc(sig("y_final"), 1)

        @block.tensor
        def _(pe):
            mm = pe.matmul
            rows4, rows1, rows2, rows3 = (scr(14336 + 128 * i, 128) for i in range(4))
            pe.wait_ge(sig("consts_loaded"), 16)
            p = fill(pe, "cond")
            pe.wait_ge(sig("cond_ready"), 1)
            filled(pe.transpose(p[:, 0:16], rows4[0:16, :], ident[0:16, 0:16]), "cond")
            pe.wait_ge(sig("params_loaded"), 16 * 10)
            for i, (src, w) in enumerate(((rows1, 128), (rows2, 125), (rows3, 28))):
                p = fill(pe, "par", i + 1)
                filled(pe.transpose(p[:, 0:w], src[0:w, :], ident[0:w, 0:w]), "par", i + 1)

            def modulation(l, part):
                p = fill(pe, "ada", l, part)
                if l == 0 and part == 0:
                    after(pe, "cond")
                pages = range(4) if part == 0 else range(4, 12)
                for c in pages:
                    w = page(pe, ("ada", l, c))
                    for m in range(4):
                        ch = 4 * c + m
                        for k in range(DC):
                            ins = mm(p[:, 2 * ch:2 * ch + 2], w[:, k, m * 128:(m + 1) * 128], condT[:, k:16:8], start=(k == 0), stop=(k == DC - 1))
                    free_page(ins, ("ada", l, c))

            def first_norm(l):
                pe.wait_ge(sig("normed", l), NT)
                for k in range(DC):
                    p = fill(pe, "hT", l, k)
                    for t in range(NT):
                        ins = pe.transpose(p[:, t * 128:(t + 1) * 128], XN[:, t, k * 128:(k + 1) * 128], ident)
                    filled(ins, "hT", l, k)
                for k in (DC - 2, DC - 1):
                    after(pe, "hT", l, k)

            def project(w, j, *name):
                p = fill(pe, *name)
                for cols in (slice(0, NS), slice(NS, TOK)):
                    for k in range(DC):
                        ins = mm(p[:, cols], w[:, k, j * 128:(j + 1) * 128], hT[:, k, cols], start=(k == 0), stop=(k == DC - 1))
                filled(ins, *name)
                return ins

            def spread(l):
                pe.wait_ge(sig("modulated2", l), 1)
                for q, src in enumerate((MOD[:, l, 16:24, :], MOD[:, l, 40:48, :], SC2[:, l], MOD[:, l, 24:32, :])):
                    for c in range(2):
                        p = fill(pe, "bc", l, q, c)
                        for k in range(DC):
                            ins = mm(p[:, k * 128:(k + 1) * 128], src[:, k, c:c + 1].broadcast_to([128, 128]), ident, start=True, stop=True)
                        filled(ins, "bc", l, q, c)

            def out_projection(l, tag, cat):
                for i in range(2 * NT):
                    n, t = divmod(i, NT)
                    w = page(pe, (tag, n))
                    p = fill(pe, "out", l, i)
                    for k in range(DC):
                        ins = mm(p[:, 0:512], cat(k)[:, t * 128:(t + 1) * 128], w[:, k, :], start=(k == 0), stop=(k == DC - 1))
                    filled(ins, "out", l, i)
                pe.drain().then_inc(sig("mixer_out_done", l), 1)
                for n in range(2):
                    pe.sem_inc(slot_free[page_at[(tag, n)][0]], 1)

            def router(l):
                if l == 0:
                    pe.wait_ge(sig("tables_loaded"), 16 * 16)
                lg = fill(pe, "logit", l)
                for t in range(NT):
                    pe.wait_ge(sig("h2_ready", l), t + 1)
                    p = fill(pe, "h2T", l, t)
                    for k in range(DC):
                        ins = pe.transpose(p[:, k * 128:(k + 1) * 128], H2[t % 2][:, k:D:DC], ident)
                    filled(ins, "h2T", l, t)
                    after(pe, "h2T", l, t)
                    for k in range(DC):
                        ins = mm(lg[:, 36 * t:36 * t + 36], H2T[t % 2][:, k, :], WR[:, l, k, :], start=(k == 0), stop=(k == DC - 1))
                    if t < NT - 1:
                        ins.then_inc(sig("tile_routed", l), 1)
                filled(ins, "logit", l)
                pe.wait_ge(sig("chosen", l), 1)
                both = scr(BOTH_AT, NT * NE)
                p = fill(pe, "rank", l)
                for t in range(NT):
                    for s in range(t + 1):
                        mm(p[:, NE * t:NE * (t + 1)], strict if s == t else ones, both[:, NE * s:NE * (s + 1)], start=(s == 0), stop=(s == t))
                for t in range(NT):
                    ins = mm(p[:, 160:192], ones, both[:, NE * t:NE * (t + 1)], start=(t == 0), stop=(t == NT - 1))
                filled(ins, "rank", l)
                pe.wait_ge(sig("one_hots", l), 1)
                p = fill(pe, "table", l)
                for i in range(10):
                    ins = mm(p[0:CAP, 0:2 * NBLK], POSH[:, i, :], VAL[:, i].rearrange("p s b -> p (s b)"), start=(i == 0), stop=(i == 9))
                filled(ins, "table", l)

            def experts(l):
                fulls = moe_base[l][0]

                def turn_rows(par, ins_sem):
                    for k in range(DC):
                        at = (k // 4) * 512 + (k % 4) * CAP
                        ins = pe.transpose(PB[A_][:, at:at + CAP], XG[par][0:CAP, k:D:DC], ident[0:CAP, 0:CAP])
                    ins.then_inc(ins_sem, 1)

                def gate_up(s0, par, half):
                    wg, wu = (slot(s0 + i).rearrange("p (k n) -> p k n", k=DC) for i in range(2))
                    for j in (2 * half, 2 * half + 1):
                        for i, w in enumerate((wg, wu)):
                            at = 512 * half + (2 * i + j % 2) * CAP
                            for k in range(DC):
                                ins = mm(PB[B_][:, at:at + CAP], w[:, k, j * 128:(j + 1) * 128],
                                         XGT[par][:, k * CAP:(k + 1) * CAP], start=(k == 0), stop=(k == DC - 1))
                    return ins

                def down(s0, par, n, gate=None):
                    wd = slot(s0 + 2).rearrange("p (j n) -> p j n", j=HC)
                    for j in range(HC):
                        if j == 2 and gate is not None:
                            gate()
                        ins = mm(PB[C_][0:CAP, n * 512:(n + 1) * 512], HIDT[par][:, j * CAP:(j + 1) * CAP], wd[:, j, n * 512:(n + 1) * 512],
                                 start=(j == 0), stop=(j == HC - 1))
                    return ins

                def body(b, par, fill_no, first, last, gath):
                    s0 = 3 * par
                    for kind in range(2):
                        pe.wait_ge(slot_full[s0 + kind], fill_no(s0 + kind))
                    pe.wait_ge(sig("x_ready", l), b + 1)
                    if not first:
                        pe.wait_ge(sig("hidden", l), 2 * b)
                    for half in range(2):
                        gate_up(s0, par, half).then_inc(sig("gate_up_done", l), 1)
                    if not last:
                        pe.wait_ge(sig("gathered", l, 1 - par), gath)
                        turn_rows(1 - par, sig("x_turned", l))
                    pe.wait_ge(slot_full[s0 + 2], fill_no(s0 + 2))
                    pe.wait_ge(sig("hidden", l), 2 * b + 1)
                    if not first:
                        pe.wait_ge(sig("y_left", l), b)
                        pe.wait_ge(sig("y_right", l), b)
                    down(s0, par, 0, lambda: pe.wait_ge(sig("hidden", l), 2 * b + 2)).then_inc(sig("down_done", l), 1)
                    down(s0, par, 1).then_inc(sig("down_done", l), 1)

                pe.wait_ge(sig("gathered", l, 0), 16)
                turn_rows(0, sig("x_turned", l))
                body(0, 0, lambda s: 16 * (fulls[s] + 1), True, False, 16)
                body(1, 1, lambda s: 16 * (fulls[s] + 1), False, False, 32)
                with nc.Fori(1, NE // 2 - 1, engines=(PE,)) as it:
                    for par in range(2):
                        body(2 * it + par, par, lambda s: 16 * it + 16 * (fulls[s] + 1), False, False, 16 * it + 16 + 16 * par)
                body(NE - 2, 0, lambda s: 16 * (fulls[s] + NE // 2), False, False, 8 * NE)
                body(NE - 1, 1, lambda s: 16 * (fulls[s] + NE // 2), False, True, None)
                pe.wait_ge(sig("y_left", l), NE)
                pe.wait_ge(sig("y_right", l), NE)
                nb = pe.value_load(NBK[0:1, 0:1], min_val=0, max_val=OVER)
                with nc.Fori(0, OVER, engines=(PE,)) as i:
                    with pe.If(nb > i):
                        pe.wait_ge(sig("more_gathered", l), 16 * i + 16)
                        turn_rows(0, sig("more_turned", l))
                        pe.wait_ge(sig("more_x_ready", l), i + 1)
                        pe.wait_ge(sig("more_weights", l), 48 * i + 48)
                        gate_up(0, 0, 0)
                        gate_up(0, 0, 1).then_inc(sig("more_gate_up", l), 1)
                        pe.wait_ge(sig("more_hidden", l), i + 1)
                        down(0, 0, 0)
                        down(0, 0, 1).then_inc(sig("more_down", l), 1)

            def ready_now(*name):
                pe.drain().then_inc(psum_ready[uses[name][0]], 1)

            modulation(0, 0)
            ready_now("ada", 0, 0)
            first_norm(0)
            wa, wb = page(pe, ("in_e", 0)), page(pe, ("in_e", 1))
            for j in range(HC):
                project(wa, j, "ga", j)
                project(wb, j, "gb", j)
            pe.drain().then_inc(slot_free[page_at[("in_e", 0)][0]], 1)
            pe.sem_inc(slot_free[page_at[("in_e", 1)][0]], 1)
            for c, name in ((2, "q"), (3, "k")):
                w = page(pe, ("in_e", c))
                for j in range(HC):
                    project(w, j, name, j)
                pe.drain().then_inc(slot_free[page_at[("in_e", c)][0]], 1)
            for name, src in (("q", qT), ("k", kT)):
                for j in range(HC):
                    after(pe, name, j)
                    p = fill(pe, "rot", name, j)
                    filled(mm(p[:, 0:NS], rot, src[:, j, 0:NS], start=True, stop=True), "rot", name, j)
            w = page(pe, ("in_e", 4))
            for t in range(NT):
                p = fill(pe, "v", t)
                for k in range(DC):
                    ins = mm(p[:, 0:HALF], hT[:, k, t * 128:(t + 1) * 128], w[:, k, :], start=(k == 0), stop=(k == DC - 1))
                filled(ins, "v", t)
            pe.drain().then_inc(slot_free[page_at[("in_e", 4)][0]], 1)
            pe.wait_ge(sig("cache_loaded"), 32)
            p = fill(pe, "kcT")
            for h in range(HEADS):
                ins = pe.transpose(p[:, h * 128:(h + 1) * 128], KC[:, h * 128:(h + 1) * 128], ident)
            filled(ins, "kcT")
            p = fill(pe, "kout")
            for h in range(HEADS):
                ins = pe.transpose(p[:, h * 128:(h + 1) * 128], kT[:, h, NS:], ident)
            filled(ins, "kout")
            for l, part in ((0, 1), (1, 0), (1, 1)):
                modulation(l, part)
                ready_now("ada", l, part)
            p = fill(pe, "mean")
            for cols, src in ((slice(0, NS), slice(0, NS)), (slice(NS, TOK), slice(15 + NS, 15 + TOK))):
                for j in range(HC):
                    pe.wait_ge(sig("conv_step", j), TAPS)
                    ins = mm(p[:, cols], ones, UO[:, j, src], start=(j == 0), stop=(j == HC - 1))
            filled(ins, "mean")
            p = fill(pe, "var")
            for j in range(HC):
                pe.wait_ge(sig("conv_squares"), j + 1)
                mm(p[:, 0:NS], ones, SQB[j % 2][:, 0:NS], start=(j == 0), stop=(j == HC - 1))
                ins = mm(p[:, NS:TOK], ones, SQB[j % 2][:, 15 + NS:15 + TOK], start=(j == 0), stop=(j == HC - 1))
                if j < HC - 1:
                    ins.then_inc(sig("squares_summed"), 1)
            filled(ins, "var")

            def scores(u):
                t, h = UNITS[u]
                for c in range(2):
                    p = fill(pe, "s", u, c)
                    rows = slice(c * DH, (c + 1) * DH)
                    q = qT[rows, h, t * 128:(t + 1) * 128]
                    if t < 4:
                        mm(p[:, 0:NS], q, kT[rows, h, 0:NS], start=True, stop=True)
                        filled(mm(p[:, NS:NS + PAST], q, kcT[rows, h, :], start=True, stop=True), "s", u, c)
                    else:
                        filled(mm(p[:, 0:NP], q, kT[rows, h, NS:], start=True, stop=True), "s", u, c)

            def turn(u):
                p = fill(pe, "aT", u)
                pe.wait_ge(sig("a_ready"), u + 1)
                for i in range(5 if UNITS[u][0] < 4 else 1):
                    ins = pe.transpose(p[:, i * 128:(i + 1) * 128], PR[:, u % 2, 0, i * 128:(i + 1) * 128], ident)
                filled(ins, "aT", u)

            def values(u):
                t, h = UNITS[u]
                p = fill(pe, "av", u)
                after(pe, "aT", u)
                hc = slice(h * 128, (h + 1) * 128)
                vs = [V[:, i, hc] for i in range(4)] + [VC[:, hc]] if t < 4 else [V[:, 4, hc]]
                for i, v in enumerate(vs):
                    ins = mm(p[:, 0:128], AT[:, u % 2, i * 128:(i + 1) * 128], v, start=(i == 0), stop=(i == len(vs) - 1))
                filled(ins, "av", u)

            pe.wait_ge(sig("roped"), 8)
            NU = len(UNITS)
            for i in range(NU + 2):
                if i < NU:
                    scores(i)
                if 1 <= i <= NU:
                    turn(i - 1)
                if i >= 2:
                    values(i - 2)
            pe.wait_ge(sig("o_normed"), 1)
            for h in range(HEADS):
                p = fill(pe, "oT", h)
                for t in range(NT):
                    ins = pe.transpose(p[:, t * 128:(t + 1) * 128], OR[:, t, h * 128:(h + 1) * 128], ident)
                filled(ins, "oT", h)
            spread(0)
            pe.wait_ge(sig("cat_u"), HC)
            out_projection(0, "out_e", lambda k: catU[:, k, :] if k < 4 else oT[:, k - 4, :])
            router(0)
            experts(0)

            first_norm(1)
            wx, wh, wb, wc = (page(pe, ("in_o", c)) for c in range(4))
            for j in range(HC):
                project(wh, j, "hd", j)
                project(wc, j, "cg", j)
                project(wb, j, "bg", j)
                project(wx, j, "xc", j)
            pe.drain().then_inc(slot_free[page_at[("in_o", 0)][0]], 1)
            for c in range(1, 4):
                pe.sem_inc(slot_free[page_at[("in_o", c)][0]], 1)
            pe.wait_ge(sig("counts_loaded"), 32)
            for j in range(HC):
                p = fill(pe, "pool", j)
                pe.wait_ge(sig("pooled"), j + 1)
                for cols in (slice(0, NS), slice(NS, TOK)):
                    ins = mm(p[:, cols], PW[:, j, :], DP[:, j, cols], start=True, stop=True)
                filled(ins, "pool", j)
            spread(1)
            pe.wait_ge(sig("short_conv"), HC)
            for j in (2, 3):
                after(pe, "pool", j)
            out_projection(1, "out_o", lambda k: CAT[:, k, :])
            router(1)
            experts(1)


_INS = ["x_prompt", "x_sample", "cache_k", "cache_v", "c", "c_ctx", "w_ada", "b_ada", "g_norm1", "g_norm2", "g_final",
        "w_in_e", "conv_a_w", "conv_a_b", "ln_a_g", "ln_a_b", "lam_q1", "lam_k1", "lam_q2", "lam_k2", "subln_g", "w_out_e",
        "w_in_o", "pool_w", "pool_scale", "conv_d_w", "w_out_o", "w_router_g", "b_router_g", "w_router_e", "b_router_e",
        "w_gate", "w_up", "w_down"]
_OUTS = [("y_prompt", (1, 128, 1024)), ("y_sample", (1, 512, 1024)), ("new_cache_k", (1, 1, 128, 4, 2, 64)),
         ("new_cache_v", (1, 1, 128, 4, 128))]


def kernel(**inputs):
    import concourse.bacc as bacc
    from concourse.bass_utils import run_bass_kernel_spmd

    nc = bacc.Bacc("TRN2", target_bir_lowering=False, num_devices=1)
    arrays, aps = {}, {}
    for name, value in [(n, inputs[n]) for n in _INS] + list(shape_constants().items()):
        value = np.ascontiguousarray(value)
        arrays[name] = value
        aps[name] = nc.dram_tensor(name, value.shape, mybir.dt.from_np(value.dtype), kind="ExternalInput").ap()
    outs = {n: nc.dram_tensor(n, s, mybir.dt.float32, kind="ExternalOutput").ap() for n, s in _OUTS}
    build(nc, aps, outs)
    r = run_bass_kernel_spmd(nc, [arrays], core_ids=[0])
    return tuple(r.results[0][n] for n, _ in _OUTS)
```

```python
import math
from contextlib import ExitStack

import numpy as np
import concourse.bass as bass
from concourse import mybir

D, TOK, NT, DC = 1024, 640, 5, 8
NS, NP = 512, 128
HALF, HC = 512, 4
HEADS, DH, PAST = 4, 64, 128
TAPS, GRID_W, AX = 31, 64, 32
NG, EPG = 4, 8
NE = NG * EPG
CAP = 96
OVER = (2 * TOK) // (CAP + 1)
NBLK = NE + OVER
MORE = -(-TOK // CAP) - 1
NOROW = 65536.0
EPS = 1e-6
LAM_INIT = 0.8 - 0.6 * math.exp(-0.3 * 0)
SLOT = 4096
WINDOWS = (2, 4, 8, 16)


def shape_constants():
    inv = (np.float32(10000.0) ** (-np.arange(0, AX, 2, dtype=np.float32) / np.float32(AX))).astype(np.float32)
    pos = np.arange(NS)
    ar = (pos // GRID_W).astype(np.float32)[:, None] * inv[None]
    ac = (pos % GRID_W).astype(np.float32)[:, None] * inv[None]
    ang = np.concatenate([ar, ar, ac, ac], axis=1).T
    ang = np.concatenate([ang, ang], axis=0).astype(np.float32)
    rot = np.zeros((128, 128), np.float32)
    for m in range(128):
        if m % 32 < 16:
            rot[m + 16, m] = -1.0
        else:
            rot[m - 16, m] = 1.0
    strict = np.triu(np.ones((128, 128), np.float32), 1)
    square = np.concatenate([np.eye(128, dtype=np.float32), np.ones((128, 128), np.float32), strict, rot,
                             np.cos(ang), np.sin(ang), np.tile(np.array([1, 0, 0, 1], np.float32), (128, 1))], axis=1)
    edges = np.zeros((HC, 2, 8), np.float32)
    for g, w in enumerate(WINDOWS):
        p = np.arange(NP)
        cut = w / (np.minimum(p + w // 2 - 1, NP - 1) - np.maximum(p - w // 2, 0) + 1)
        edges[g, 0], edges[g, 1] = cut[:8], cut[-8:]
    iotas = np.concatenate([np.arange(NG) - 100, np.arange(EPG) - 100, np.arange(NE), np.arange(CAP),
                            np.arange(NBLK), np.arange(OVER), CAP * np.arange(1, MORE + 1)]).astype(np.float32)
    rows = np.zeros((128, 2, 2, NT), np.float32)
    tok = np.arange(NT)[None] * 128 + np.arange(128)[:, None]
    for k in range(2):
        rows[:, 0, k] = tok - NOROW
        rows[:, 1, k] = 2 * tok + k - NOROW
    return {"const_square": square, "const_edges": edges.reshape(-1), "const_iotas": iotas,
            "const_rows": rows.reshape(128, -1)}


def build(nc, a, out):
    f32, i32 = mybir.dt.float32, mybir.dt.int32
    ALU, ACT, AX_X = mybir.AluOpType, mybir.ActivationFunctionType, mybir.AxisListType.X
    SP, PE, DVE, POOL, ACTE = (mybir.EngineType.SP, mybir.EngineType.PE, mybir.EngineType.DVE,
                               mybir.EngineType.Pool, mybir.EngineType.Activation)
    ctx = ExitStack()
    with ctx:
        def sb(name, cols, dt=f32):
            return ctx.enter_context(nc.sbuf_tensor(name, [128, cols], dt))

        X = sb("x_residual", NT * D)[:, :].rearrange("p (t d) -> p t d", t=NT)
        BC = sb("gates_by_token", 4 * D)[:, :].rearrange("p (q c d) -> p q c d", q=2, c=2)
        RING = sb("weight_ring", 6 * SLOT)
        SQ = sb("square_consts", 4 * 128 + 2 * NS + 4)
        ident, ones, strict, rot = (SQ[:, i * 128:(i + 1) * 128] for i in range(4))
        cos, sin = SQ[:, 512:512 + NS], SQ[:, 512 + NS:512 + 2 * NS]
        SEL = [SQ[:, 512 + 2 * NS + 2 * c:514 + 2 * NS + 2 * c] for c in range(2)]
        NIO = NG + EPG + NE + CAP + NBLK + OVER + MORE
        IO = sb("iotas", NIO)
        o = 0
        iota = {}
        for n, w in (("g", NG), ("e", EPG), ("E", NE), ("c", CAP), ("b", NBLK), ("o", OVER), ("m", MORE)):
            iota[n] = IO[:, o:o + w]
            o += w
        ROWS = sb("row_numbers", 20)[:, :].rearrange("p (s k t) -> p s k t", s=2, k=2)
        P1 = sb("params_1", 32)
        P2 = sb("params_2", 125)
        P3 = sb("params_3", 12)
        g_n1T = P1[:, 0:16].rearrange("p (l k) -> p l k", l=2)
        conv_bT, ln_gT, ln_bT, pool_sT = (P1[:, 16 + 4 * i:20 + 4 * i] for i in range(4))
        conv_wT = P2[:, 0:124].rearrange("p (t j) -> p t j", t=TAPS)
        sublnT = P2[:, 124:125]
        sconv_wT = P3[:, 0:12].rearrange("p (t j) -> p t j", t=3)
        condT = sb("cond_T", 16)
        MOD = sb("modulation_T", 2 * 32)[:, :].rearrange("p (l s c) -> p l c s", l=2, s=2)
        SC1 = sb("scale1_T", 32)[:, :].rearrange("p (l k s) -> p l k s", l=2, k=8)
        EDG = sb("pool_edges", HC * 16)[:, :].rearrange("p (j e w) -> p j e w", j=HC, e=2)
        BF = mybir.dt.bfloat16
        strict_bf, ones_bf = sb("strict_bf", 128, BF), sb("ones_bf", 128, BF)
        CHB = sb("chosen_bf", NT * NE, BF)
        WR = sb("router_weights", 2 * DC * 36)[:, :].rearrange("p (l k n) -> p l k n", l=2, k=DC)
        BR = sb("router_bias", 72)[:, :].rearrange("p (l n) -> p l n", l=2)
        small = sb("small", 160)
        ssq, rstd = small[:, 0:5], small[:, 5:10]
        lam2, laml, lam_neg = small[:, 10:12], small[:, 12:14], small[:, 14:15]
        eps1 = small[:, 15:16]
        oss, orstd = small[:, 20:40], small[:, 40:60]
        smx, snb, sl, sr = (small[:, 60 + 4 * i:64 + 4 * i].rearrange("p (u c) -> p u c", u=2) for i in range(4))
        sub2 = small[:, 80:81]
        WT1, WT2 = small[:, 90:95], small[:, 95:100]
        IDX = sb("row_index_table", 2 * NBLK, i32)
        NBK = sb("further_blocks", 1 + OVER, i32)
        GI = [sb(f"gather_rows_{i}", 1, i32) for i in range(2)]
        SI = [sb(f"scatter_rows_{i}", 1, i32) for i in range(2)]
        SCR_N = 15872
        SCR = sb("scratch", SCR_N)

        def scr(at, n):
            assert at + n <= SCR_N
            return SCR[:, at:at + n]

        def slot(s):
            return RING[:, s * SLOT:(s + 1) * SLOT]

        free45 = RING[:, 4 * SLOT:6 * SLOT]
        hT = scr(0, DC * TOK).rearrange("p (k t) -> p k t", k=DC)
        XN = free45[:, 0:NT * D].rearrange("p (t d) -> p t d", t=NT)
        GW = BC.rearrange("p q c d -> p (q c d)")
        ACC = GW[:, 2048:4096].rearrange("p (u c n) -> p u c n", u=2, c=2)
        UPW, UOW = 15 * 3 + TOK, 15 + TOK
        LATE = HC * UPW
        INI = [[GW[:, 512 * i:512 * i + 512] for i in range(2)], [free45[:, LATE + 512 * i:LATE + 512 * i + 512] for i in range(2)]]
        MROW, GROW = GW[0:2, 1024:1536], GW[0:2, 1536:2048]
        MALL, PE_BIAS = GW[:, 1024:1536], [GW[:, 1536:2048], scr(5120, 512)]
        qT = scr(5120, HC * TOK).rearrange("p (h t) -> p h t", h=HC)
        kT = scr(7680, HC * TOK).rearrange("p (h t) -> p h t", h=HC)
        V = scr(10240, NT * HALF).rearrange("p (t n) -> p t n", t=NT)
        KC = scr(12800, HALF)
        kcT = scr(13312, HALF).rearrange("p (h t) -> p h t", h=HC)
        VC = scr(13824, HALF)
        GA = scr(14336, TOK)
        SG = scr(14976, TOK)
        AT = scr(14336, 2 * TOK).rearrange("p (u t) -> p u t", u=2)
        LAMV = scr(15616, 4 * DH)
        UP = free45[:, 0:HC * UPW].rearrange("p (j w) -> p j w", j=HC)
        UO = free45[:, HC * UPW:HC * (UPW + UOW)].rearrange("p (j w) -> p j w", j=HC)
        assert HC * (UPW + UOW) + HC * TOK <= 2 * SLOT
        catU = free45[:, HC * (UPW + UOW):HC * (UPW + UOW) + HC * TOK].rearrange("p (j t) -> p j t", j=HC)
        QC, RQ = catU[:, 0, 0:NS], catU[:, 1, 0:NS]
        QZ = free45[:, 0:HC * TOK].rearrange("p (h t) -> p h t", h=HC)
        MU, RS = scr(14336, UOW), scr(14336 + UOW, UOW)
        SQB = [scr(i * UOW, UOW) for i in range(2)]
        PR = scr(0, 4 * TOK).rearrange("p (u c t) -> p u c t", u=2, c=2)
        OR = scr(2560, NT * HALF).rearrange("p (t n) -> p t n", t=NT)
        oT = scr(5120, HC * TOK).rearrange("p (h t) -> p h t", h=HC)
        XPW = 8 * 3 + TOK
        TPW = 3 + TOK
        XP = scr(5120, XPW)
        PS2 = [scr(5800 + 700 * i, XPW) for i in range(2)]
        DP = scr(7200, 2 * TOK).rearrange("p (u t) -> p u t", u=2)
        HD = scr(8480, TOK)
        CG = scr(9120, TOK)
        TP = scr(9760, HC * 650).rearrange("p (j w) -> p j w", j=HC)
        CA = scr(12360, TPW)
        BG = scr(13010, TOK)
        PW = scr(13650, HC * 128).rearrange("p (j e) -> p j e", j=HC)
        CAT = free45[:, 0:DC * TOK].rearrange("p (k t) -> p k t", k=DC)
        M2 = scr(0, 4 * D).rearrange("p (q c d) -> p q c d", q=2, c=2)
        H2 = [scr(7680 + D * i, D) for i in range(NT)]
        H2T = [scr(at, D).rearrange("p (k t) -> p k t", k=DC) for at in (4096, 13824)]
        TMP = scr(14848, 512)
        XG = H2[0:2]
        XGT = [scr(DC * CAP * i, DC * CAP) for i in range(2)]
        HIDT = [scr(2 * DC * CAP + HC * CAP * i, HC * CAP) for i in range(2)]
        SIL = scr(2 * DC * CAP + 2 * HC * CAP, HC * CAP)
        YR_AT = 2 * DC * CAP + 3 * HC * CAP
        YR = [scr(YR_AT + D * i, D) for i in range(2)]
        POSH_AT = YR_AT + 2 * D
        POSH = scr(POSH_AT, 10 * CAP).rearrange("p (a c) -> p a c", a=10)
        VAL = scr(POSH_AT + 10 * CAP, 20 * NBLK).rearrange("p (s a b) -> p s a b", s=2, a=10)
        EQB = scr(POSH_AT + 10 * CAP + 20 * NBLK, 10 * NBLK).rearrange("p (a b) -> p a b", a=10)
        assert POSH_AT + 10 * CAP + 30 * NBLK <= 7680
        RT = 12800
        YB = [scr(2 * D * i, 2 * D) for i in range(NT)]
        GF = scr(10240, D)

        PB = [ctx.enter_context(nc.psum_tensor(f"psum_pair_{n}", [128, 1024], f32)) for n in "ABCD"]
        A_, B_, C_, D_ = range(4)
        HALVES = PB[B_][:, :].rearrange("p (h c) -> p h c", h=2)
        h2_dram = nc.dram_tensor("h2_rows", [TOK, D], f32, kind="Internal").ap()
        mod_dram = nc.dram_tensor("modulation_rows", [2, 2, 6 * D], f32, kind="Internal").ap()
        y_dram = nc.dram_tensor("expert_rows", [2 * TOK, D], f32, kind="Internal").ap()

        sems = {}

        def sig(name, *at):
            key = "_".join([name, *map(str, at)])
            if key not in sems:
                sems[key] = ctx.enter_context(nc.semaphore(key))
            return sems[key]

        slot_full = [sig("slot_full", s) for s in range(6)]
        psum_ready = [sig("psum_ready", p) for p in range(4)]
        psum_taken = [sig("psum_taken", p) for p in range(4)]

        def ada(l, c):
            return ("ada", l, c), a["w_ada"][l].rearrange("(k p) n -> p k n", p=128)[:, :, c * 512:(c + 1) * 512]

        def mix(tag, c):
            w = {"in_e": a["w_in_e"], "out_e": a["w_out_e"], "in_o": a["w_in_o"], "out_o": a["w_out_o"]}[tag][0]
            return (tag, c), w.rearrange("(k p) n -> p k n", p=128)[:, :, c * 512:(c + 1) * 512]

        dense = [[(0, ada(0, 0)), (1, ada(0, 1)), (2, ada(0, 2)), (3, ada(0, 3)),
                  (0, mix("in_e", 0)), (1, mix("in_e", 1)), (2, ada(0, 4)), (3, ada(0, 5)),
                  (2, mix("in_e", 2)), (3, mix("in_e", 3)), (0, ada(0, 6)), (1, ada(0, 7)), (2, mix("in_e", 4)),
                  (0, ada(0, 8)), (1, ada(0, 9)), (3, ada(0, 10)), (0, ada(0, 11)),
                  (2, mix("out_e", 0)), (3, mix("out_e", 1)),
                  (1, ada(1, 0)), (0, ada(1, 1)), (1, ada(1, 2)), (0, ada(1, 3))],
                 [(0, mix("in_o", 0)), (1, mix("in_o", 1)), (2, mix("in_o", 3)), (3, ada(1, 4)), (3, ada(1, 5)),
                  (3, ada(1, 6)), (0, ada(1, 7)), (3, ada(1, 8)), (0, mix("in_o", 2)), (3, ada(1, 9)),
                  (3, ada(1, 10)), (1, mix("out_o", 0)), (2, mix("out_o", 1)), (3, ada(1, 11))]]
        PRODUCTS_AT = {"xc": ((), (4,), (), (5,)), "cg": ((6,), (7,), (8,), (9,)), "bg": ((10,), (11,), (), ())}
        SUMS_AT = {"xc": ((), (), (), (4,)), "cg": ((5,), (6,), (7,), (8,)), "bg": ((9,), (), (10,), (11,))}
        ADA_OPS = 2 * DC
        freed, n_ada, n_mix = {}, 0, 0
        for tag, c in [("in_e", c) for c in (0, 1, 2, 3, 4)] + [("out_e", 0), ("out_e", 1)] + \
                      [("in_o", c) for c in (0, 1, 3, 2)] + [("out_o", 0), ("out_o", 1)]:
            n_mix += 1
            freed[(tag, c)] = (sig("mixer_page_used"), n_mix)
        ON_PE = (1, 3)
        ADA_ORDER = [(0, c) for c in range(12) if c not in ON_PE] + [(1, c) for c in range(12)]
        ADA_NO = {name: n for n, name in enumerate(ADA_ORDER)}
        for l, c in ADA_ORDER:
            n_ada += 1
            freed[("ada", l, c)] = (sig("row_product"), ADA_OPS * n_ada)
        for n, c in enumerate(ON_PE):
            freed[("ada", 0, c)] = (sig("ada_page_used"), n + 1)
        page_at, fills, owner = {}, [0] * 6, [None] * 6
        moe_base, plan = [], []
        for l in range(2):
            for s, (name, src) in dense[l]:
                page_at[name] = (s, fills[s] + 1)
                plan.append((l, name, src, s, owner[s]))
                fills[s] += 1
                owner[s] = name
            moe_base.append((list(fills), list(owner)))
            fills = [f + NE // 2 for f in fills]
            owner = ["expert"] * 4

        def page(eng, name):
            s, n = page_at[name]
            eng.wait_ge(slot_full[s], 16 * n)
            return slot(s).rearrange("p (k n) -> p k n", k=DC)

        uses, count = {}, [0] * 4

        def put(pair, *name):
            uses[name] = (pair, count[pair])
            count[pair] += 1

        def put_ab(names):
            for i, n in enumerate(names):
                put(i % 2, *n)

        UNITS = [(t, h) for t in range(4) for h in range(HEADS)] + [(4, h) for h in range(HEADS)]
        put(D_, "cond")
        for c in range(4):
            if c in ON_PE:
                put(D_, "row", 0, c)
            put(C_, "adaT", 0, c)
            if c == 1:
                put(A_, "par", 1), put(B_, "par", 2), put(C_, "par", 3)
        put_ab([("hT", 0, k) for k in range(DC)])
        for j in range(HC):
            put(A_, "ga", j), put(B_, "gb", j)
            if j == 1:
                put(C_, "row", 0, 4), put(D_, "row", 0, 5)
        put_ab([("q", j) for j in range(HC)])
        put_ab([("k", j) for j in range(HC)])
        VALUES_ORDER = [("v", 0), ("rot", "q", 0), ("rot", "q", 1), ("v", 1), ("rot", "q", 2), ("rot", "q", 3), ("row", 0, 6),
                        ("v", 2), ("rot", "k", 0), ("rot", "k", 1), ("row", 0, 7), ("v", 3), ("rot", "k", 2), ("rot", "k", 3),
                        ("v", 4), ("row", 0, 8)]
        for name in VALUES_ORDER:
            put({"v": (A_, B_), "rot": (C_, D_), "row": (C_, D_)}[name[0]][name[-1] % 2], *name)
        put(C_, "mean"), put(B_, "var")
        put(D_, "row", 0, 9)
        put(C_, "kcT"), put(D_, "kout")
        put(C_, "row", 0, 10)
        SUMS_AT_UNIT = {3: ("row", 0, 11), 11: ("adaT", 1, 0), 19: ("adaT", 1, 1)}
        for u in range(len(UNITS) + 1):
            if u < len(UNITS):
                put(A_, "s", u, 0), put(B_, "s", u, 1), put(D_, "av", u)
            if u:
                put(C_, "aT", u - 1)
            if u in SUMS_AT_UNIT:
                put(C_, *SUMS_AT_UNIT[u])
        put_ab([("oT", h) for h in range(HEADS)])

        def put_tail(l):
            for t in range(NT):
                put(C_, "out", l, t, 0), put(D_, "out", l, t, 1)
                if t:
                    put((A_, B_)[(t - 1) % 2], "h2T", l, t - 1)
                if l == 0 and t >= 3:
                    put(C_, "adaT", 1, t - 1)
            put((A_, B_)[(NT - 1) % 2], "h2T", l, NT - 1)
            put(D_, "logit", l)
            put(C_, "rank", l), put(D_, "table", l)

        put_tail(0)
        put_ab([("hT", 1, k) for k in range(DC)])
        for j in range(HC):
            put((A_, B_)[j % 2], "xc", j)
            put(C_, "pool", j)
            for c in SUMS_AT["xc"][j]:
                put(D_, "row", 1, c)
        for j in range(HC):
            put(A_, "hd", j), put(B_, "cg", j)
            for c in SUMS_AT["cg"][j]:
                put(D_, "row", 1, c)
        for j in range(HC):
            put((A_, B_)[j % 2], "bg", j)
            for c in SUMS_AT["bg"][j]:
                put(D_, "row", 1, c)
        put_tail(1)

        def fill(eng, *name):
            p, n = uses[name]
            if n:
                eng.wait_ge(psum_taken[p], n)
            return PB[p]

        def filled(ins, *name):
            ins.then_inc(psum_ready[uses[name][0]], 1)

        def take(eng, *name):
            p, n = uses[name]
            eng.wait_ge(psum_ready[p], n + 1)
            return PB[p]

        def took(ins, *name):
            ins.then_inc(psum_taken[uses[name][0]], 1)

        def after(eng, *name):
            p, n = uses[name]
            eng.wait_ge(psum_taken[p], n + 1)

        def chain(eng, name):
            s, n = sig(name), [0]

            def link(ins):
                ins.then_inc(s, 1)
                n[0] += 1
                eng.wait_ge(s, n[0])
            return link

        def cond_of(t):
            return 0 if t < 4 else 1

        block = ctx.enter_context(nc.Block())

        @block.sync
        def _(sp):
            sp.wait_ge(sig("cond_loaded"), 32)

            def bias_row(l, c):
                if l == 0 and c in ON_PE:
                    sp.dma_start(PE_BIAS[ON_PE.index(c)][0:1, :], a["b_ada"][l:l + 1, c * 512:(c + 1) * 512]).then_inc(sig("bias_for_pe", ON_PE.index(c)), 16)
                    return
                n = ADA_NO[(l, c)]
                if n >= 2:
                    sp.wait_ge(sig("row_product"), ADA_OPS * (n - 1))
                where = INI[1 if (l, c // 4) == (1, 0) else 0][n % 2]
                sp.dma_start(where[0:1, :], a["b_ada"][l:l + 1, c * 512:(c + 1) * 512]).then_inc(sig("bias_row", n % 2), 16)

            rows = y_dram.rearrange("(t p two) d -> t p (two d)", p=128, two=2)

            def expert_rows(l, t):
                sp.dma_start(YB[t], rows[t]).then_inc(sig("y_back", t), 16)

            for l in range(2):
                for i, (_, name, src, s, before) in enumerate(p for p in plan if p[0] == l):
                    if l == 1 and i == 3:
                        sp.wait_ge(sig("experts_done", 0), 1)
                        for t in range(NT):
                            expert_rows(0, t)
                    if before == "expert":
                        sp.wait_ge(sig("down_done" if s == 2 else "gate_up_done", 0), 2 * NE if s == 3 else 2 * (NE - 1))
                    elif before is not None:
                        sp.wait_ge(*freed[before])
                    if name[0] == "ada":
                        if name[1:] == (0, 0):
                            sp.wait_ge(sig("starts_zero"), 1)
                        if name[1:] == (1, 0):
                            sp.wait_ge(sig("starts_zero"), 2)
                        if name[1:] == (1, 4):
                            sp.wait_ge(sig("starts_zero"), 3)
                        bias_row(*name[1:])
                    sp.dma_start(slot(s).rearrange("p (k n) -> p k n", k=DC), src).then_inc(slot_full[s], 16)
                    if name == ("ada", 0, 1):
                        sp.dma_start(X[:, 0:4, :], a["x_sample"][0].rearrange("(t p) d -> p t d", p=128)).then_inc(sig("x_loaded"), 16)
                        sp.dma_start(X[:, 4, :], a["x_prompt"][0]).then_inc(sig("x_loaded"), 16)
                wg, wu = a["w_gate"][l], a["w_up"][l]
                wd = a["w_down"][l]

                def gate_page(w, e):
                    return w[bass.ds(e, 1)].rearrange("a (p k) n -> p (a k n)", k=DC)

                def down_page(e):
                    return wd[bass.ds(e, 1)].rearrange("a (j p) n -> (a p) j n", p=128)

                def expert(e, par, first):
                    for kind, w in enumerate((wg, wu, wd)):
                        s = 3 * par + kind
                        if first:
                            if s < 4:
                                sp.wait_ge(*freed[moe_base[l][1][s]])
                            elif s == 4:
                                sp.wait_ge(sig("mixer_out_done"), l + 1)
                        elif kind != 1:
                            sp.wait_ge(sig("gate_up_done" if kind == 0 else "down_done", l), 2 * e - 2)
                        if kind < 2:
                            sp.dma_start(slot(s), gate_page(w, e)).then_inc(slot_full[s], 16)
                        else:
                            sp.dma_start(slot(s).rearrange("p (j n) -> p j n", j=HC), down_page(e)).then_inc(slot_full[s], 16)

                expert(0, 0, True)
                expert(1, 1, True)
                with nc.Fori(1, NE // 2, engines=(SP,)) as it:
                    for par in range(2):
                        expert(2 * it + par, par, False)
                sp.wait_ge(sig("routed"), l + 1)
                nb = sp.value_load(NBK[0:1, 0:1], min_val=0, max_val=OVER)
                with sp.If(nb > 0):
                    with nc.Fori(0, OVER, engines=(SP,)) as i:
                        with sp.If(nb > i):
                            e = sp.value_load(NBK[0:1, bass.ds(i + 1, 1)], min_val=0, max_val=NE - 1)
                            sp.wait_ge(sig("down_done", l), 2 * NE)
                            sp.dma_start(slot(0), gate_page(wg, e)).then_inc(sig("more_weights", l), 16)
                            sp.dma_start(slot(1), gate_page(wu, e)).then_inc(sig("more_weights", l), 16)
                            sp.dma_start(slot(2).rearrange("p (j n) -> p j n", j=HC), down_page(e)).then_inc(sig("more_weights", l), 16)
                            sp.wait_ge(sig("more_down", l), i + 1)
                            sp.sem_inc(sig("more_slots_back"), 1)
            sp.wait_ge(sig("experts_done", 1), 1)
            for t in range(NT):
                expert_rows(1, t)

        @block.gpsimd
        def _(pool):
            link = chain(pool, "pool_step")
            starts = GW[:, 0:1024]
            pool.memset(PE_BIAS[1], 0.0)
            pool.memset(GW[:, 0:2048], 0.0).then_inc(sig("starts_zero"), 1)

            def rows_out(l, c):
                after(pool, "row", l, c)
                if c in (8, 9):
                    pool.wait_ge(sig("gain_row"), 16 * (2 * l + c - 7))
                    link(pool.tensor_scalar(MROW, MROW, 1.0, None, ALU.add))
                    link(pool.tensor_tensor(MROW, MROW, GROW, ALU.mult))
                pool.dma_start(mod_dram[l, :, c * 512:(c + 1) * 512], MROW).then_inc(sig("rows_stored"), 16)

            for k in (6, 7):
                after(pool, "hT", 0, k)
            for j in range(HC):
                for at in (0, 15 + NS, 30 + TOK):
                    ins = pool.memset(UP[:, j, at:at + 15], 0.0)
            link(ins)
            for j in range(HC):
                after(pool, "ga", j)
                after(pool, "gb", j)
                pool.tensor_tensor(UP[:, j, 15:15 + NS], GA[:, 0:NS], SG[:, 0:NS], ALU.mult)
                pool.tensor_tensor(UP[:, j, 30 + NS:30 + TOK], GA[:, NS:], SG[:, NS:], ALU.mult).then_inc(sig("u_ready"), 1)
                if j == 1:
                    rows_out(0, 4)
                    rows_out(0, 5)
            for name, dst in (("q", qT), ("k", kT)):
                for j in range(HC):
                    if (name, j) == ("k", 0):
                        rows_out(0, 6)
                    if (name, j) == ("k", 2):
                        rows_out(0, 7)
                    after(pool, "rot", name, j)
                    pool.tensor_tensor(QC, dst[:, j, 0:NS], cos, ALU.mult)
                    link(pool.tensor_tensor(RQ, RQ, sin, ALU.mult))
                    pool.tensor_tensor(dst[:, j, 0:NS], QC, RQ, ALU.add).then_inc(sig("roped"), 1)
            rows_out(0, 8)
            pool.wait_ge(sig("roped"), 8)
            pool.wait_ge(sig("conv_step", HC - 1), TAPS)
            pool.memset(QZ[0:DH], 0.0)
            link(pool.tensor_copy(QZ[DH:128], qT[DH:128]))
            pool.memset(qT[DH:128], 0.0).then_inc(sig("queries_ready"), 1)
            pool.wait_ge(sig("queries_ready"), 1)
            rows_out(0, 9)
            rows_out(0, 10)
            pool.wait_ge(sig("cat_u"), HC)
            pool.memset(free45[:, LATE:LATE + 1024], 0.0).then_inc(sig("starts_zero"), 1)
            rows_out(0, 11)

            for l in range(2):
                if l == 1:
                    pool.wait_ge(sig("combined", 0), NT)
                    pool.memset(starts, 0.0).then_inc(sig("starts_zero"), 1)
                    for at in (0, 8 + NS, 16 + TOK):
                        pool.memset(XP[:, at:at + 8], 0.0)
                    for at in (0, 1 + NS, 2 + TOK):
                        ins = pool.memset(TP[:, :, at:at + 1], 0.0)
                    ins.then_inc(sig("pads_zero"), 1)
                    for c in range(4, 12):
                        rows_out(1, c)
                pool.wait_ge(sig("routed"), l + 1)
                pool.wait_ge(sig("h2_stored"), 16 * NT * (l + 1))
                gathered = [sig("gathered", l, i) for i in range(2)]
                scattered = [sig("scattered", l, i) for i in range(2)]
                copied = sig("rows_copied", l)

                def gather(b, par, turns, steps):
                    if turns is not None:
                        pool.wait_ge(sig("x_turned", l), turns)
                        pool.sem_inc(sig("gather_issued"), 1)
                    pool.tensor_copy(GI[par][0:CAP, :], IDX[0:CAP, bass.ds(b, 1)]).then_inc(copied, 1)
                    pool.wait_ge(copied, steps)
                    pool.sem_inc(sig("gather_issued"), 1)
                    pool.indirect_dma_start(XG[par][0:CAP, :], None, h2_dram, bass.IndirectOffsetOnAxis(GI[par][0:CAP, :], 0),
                                            bounds_check=TOK - 1, oob_is_err=False).then_inc(gathered[par], 16)

                def scatter(b, par, before, steps):
                    if before is not None:
                        pool.wait_ge(scattered[par], before)
                    pool.sem_inc(sig("scatter_issued"), 1)
                    pool.tensor_copy(SI[par][0:CAP, :], IDX[0:CAP, bass.ds(b + NBLK, 1)]).then_inc(copied, 1)
                    pool.wait_ge(copied, steps)
                    pool.wait_ge(sig("y_left", l), b + 1)
                    pool.wait_ge(sig("y_right", l), b + 1)
                    pool.sem_inc(sig("scatter_issued"), 1)
                    pool.indirect_dma_start(y_dram, bass.IndirectOffsetOnAxis(SI[par][0:CAP, :], 0), YR[par][0:CAP, :], None,
                                            bounds_check=2 * TOK - 1, oob_is_err=False).then_inc(scattered[par], 16)

                gather(0, 0, None, 1)
                gather(1, 1, None, 2)
                gather(2, 0, 1, 3)
                scatter(0, 0, None, 4)
                gather(3, 1, 2, 5)
                scatter(1, 1, None, 6)
                with nc.Fori(1, NE // 2 - 1, engines=(POOL,)) as it:
                    for par in range(2):
                        b = 2 * it + par
                        gather(b + 2, par, b + 1, 4 * it + 2 * par + 3)
                        scatter(b, par, 16 * it, 4 * it + 2 * par + 4)
                scatter(NE - 2, 0, 8 * NE - 16, 2 * NE - 1)
                scatter(NE - 1, 1, 8 * NE - 16, 2 * NE)
                for i in range(2):
                    pool.wait_ge(scattered[i], 8 * NE)
                nb = pool.value_load(NBK[0:1, 0:1], min_val=0, max_val=OVER)
                with pool.If(nb > 0):
                    with nc.Fori(0, OVER, engines=(POOL,)) as i:
                        with pool.If(nb > i):
                            pool.tensor_copy(GI[0][0:CAP, :], IDX[0:CAP, bass.ds(i + NE, 1)])
                            pool.tensor_copy(SI[0][0:CAP, :], IDX[0:CAP, bass.ds(i + NE + NBLK, 1)]).then_inc(sig("more_copied", l), 1)
                            pool.wait_ge(sig("more_copied", l), i + 1)
                            pool.sem_inc(sig("gather_issued"), 1)
                            pool.indirect_dma_start(XG[0][0:CAP, :], None, h2_dram, bass.IndirectOffsetOnAxis(GI[0][0:CAP, :], 0),
                                                    bounds_check=TOK - 1, oob_is_err=False).then_inc(sig("more_gathered", l), 16)
                            pool.wait_ge(sig("more_left", l), i + 1)
                            pool.wait_ge(sig("more_right", l), i + 1)
                            pool.sem_inc(sig("scatter_issued"), 1)
                            pool.indirect_dma_start(y_dram, bass.IndirectOffsetOnAxis(SI[0][0:CAP, :], 0), YR[0][0:CAP, :], None,
                                                    bounds_check=2 * TOK - 1, oob_is_err=False).then_inc(sig("more_scattered", l), 16)
                            pool.wait_ge(sig("more_scattered", l), 16 * i + 16)
                            pool.sem_inc(sig("more_done"), 1)
                pool.sem_inc(sig("experts_done", l), 1)
                for t in range(NT):
                    pool.wait_ge(sig("y_gated"), NT * l + t + 1)
                    pool.tensor_tensor(X[:, t, :], X[:, t, :], YB[t][:, 0:D], ALU.add).then_inc(sig("combined", l), 1)

        @block.scalar
        def _(act):
            link = chain(act, "act_step")
            rows4, rows1, rows2, rows3 = (scr(14336 + 128 * i, 128) for i in range(4))
            act.dma_start(rows4[0:8, :], a["c"][0].rearrange("(k p) -> k p", p=128)).then_inc(sig("cond_loaded"), 16)
            act.dma_start(rows4[8:16, :], a["c_ctx"].rearrange("(k p) -> k p", p=128)).then_inc(sig("cond_loaded"), 16)
            act.dma_start(SQ[:, :], a["const_square"]).then_inc(sig("consts_loaded"), 16)
            act.wait_ge(sig("cond_loaded"), 32)
            act.activation(rows4[0:16, :], rows4[0:16, :], ACT.Silu).then_inc(sig("cond_ready"), 1)
            n = 0
            for dst, parts in ((rows1, [a["g_norm1"].rearrange("l (c p) -> (l c) p", p=128),
                                        a["conv_a_b"].rearrange("l (c p) -> (l c) p", p=128), a["ln_a_g"].rearrange("l (c p) -> (l c) p", p=128),
                                        a["ln_a_b"].rearrange("l (c p) -> (l c) p", p=128), a["pool_scale"].rearrange("l (c p) -> (l c) p", p=128)]),
                               (rows2, [a["conv_a_w"][0].rearrange("t (c p) -> (t c) p", p=128), a["subln_g"]]),
                               (rows3, [a["conv_d_w"][0].rearrange("t (c p) -> (t c) p", p=128)])):
                at = 0
                for src in parts:
                    m = src.shape[0]
                    act.dma_start(dst[at:at + m, :], src).then_inc(sig("params_loaded"), 16)
                    at += m
                    n += 1
            for i, nm in enumerate(("lam_q1", "lam_k1", "lam_q2", "lam_k2")):
                act.dma_start(LAMV[:, i * DH:(i + 1) * DH], a[nm][0].partition_broadcast(128)).then_inc(sig("lam_loaded"), 16)

            def tables_and_caches():
                act.dma_start(IO[:, :], a["const_iotas"].partition_broadcast(128)).then_inc(sig("tables_loaded"), 16)
                act.dma_start(ROWS.rearrange("p s k t -> p (s k t)"), a["const_rows"]).then_inc(sig("tables_loaded"), 16)
                act.dma_start(EDG.rearrange("p j e w -> p (j e w)"), a["const_edges"].partition_broadcast(128)).then_inc(sig("tables_loaded"), 16)
                for l in range(2):
                    act.dma_start(WR[:, l, :, 0:NG], a["w_router_g"][l].rearrange("(p k) g -> p k g", k=DC)).then_inc(sig("tables_loaded"), 16)
                    for g in range(NG):
                        act.dma_start(WR[:, l, :, NG + g * EPG:NG + (g + 1) * EPG],
                                      a["w_router_e"][l, g].rearrange("(p k) e -> p k e", k=DC)).then_inc(sig("tables_loaded"), 16)
                    act.dma_start(BR[:, l, 0:NG], a["b_router_g"][l].partition_broadcast(128)).then_inc(sig("tables_loaded"), 16)
                    act.dma_start(BR[:, l, NG:36], a["b_router_e"][l].rearrange("g e -> (g e)").partition_broadcast(128)).then_inc(sig("tables_loaded"), 16)
                act.dma_start(KC, a["cache_k"].rearrange("b l t h c d -> (b l t) (h c d)")).then_inc(sig("cache_loaded"), 16)
                act.dma_start(VC, a["cache_v"].rearrange("b l t h c -> (b l t) (h c)")).then_inc(sig("cache_loaded"), 16)

            def norm_tile(t, junk):
                n = NORM[0]
                NORM[0] += 1
                act.activation(junk, X[:, t, :], ACT.Square, accum_out=ssq[:, t:t + 1]).then_inc(sig("squares_done"), 1)
                act.wait_ge(sig("mean_square"), n + 1)
                act.activation(rstd[:, t:t + 1], rstd[:, t:t + 1], ACT.Sqrt).then_inc(sig("root_done"), 1)

            NORM = [0]

            def first_norm(l):
                if l == 0:
                    first_pages(0, 1)
                for t in range(NT):
                    if l == 0:
                        act.wait_ge(sig("x_loaded"), 32)
                    else:
                        act.wait_ge(sig("combined", 0), t + 1)
                    norm_tile(t, XN[:, t, :])
                if l == 0:
                    first_pages(2, 3)
                for k in range(0, DC, 2):
                    p = take(act, "hT", l, k)
                    if k == 0:
                        act.wait_ge(sig("modulated", l), 1)
                    act.activation(hT[:, k, 0:NS], p[:, 0:NS], ACT.Identity, bias=MOD[:, l, k, 0:1], scale=SC1[:, l, k, 0:1])
                    took(act.activation(hT[:, k, NS:], p[:, NS:TOK], ACT.Identity, bias=MOD[:, l, k, 1:2], scale=SC1[:, l, k, 1:2]), "hT", l, k)

            def first_pages(*pages):
                for c in pages:
                    if c in ON_PE:
                        p = take(act, "row", 0, c)
                        act.wait_ge(sig("starts_zero"), 1)
                        if c != ON_PE[0]:
                            take(act, "adaT", 0, ON_PE[0])
                        took(act.activation(MROW, p[0:2, 0:512], ACT.Copy), "row", 0, c)
                    shift_and_scale(0, [c])

            def shift_and_scale(l, pages):
                for c in pages:
                    p = take(act, "adaT", l, c)
                    took(act.activation(MOD[:, l, 4 * c:4 * c + 4, :], p[:, 0:8].rearrange("p (m s) -> p m s", s=2), ACT.Copy), "adaT", l, c)

            def modulation_row(l, c, n):
                p = take(act, "row", l, c)
                if n:
                    act.wait_ge(sig("rows_stored"), 16 * n)
                if c in (8, 9):
                    act.dma_start(GROW, a["g_norm2"][l, (c - 8) * 512:(c - 7) * 512].partition_broadcast(2)).then_inc(sig("gain_row"), 16)
                took(act.activation(MROW, p[0:2, 0:512], ACT.Copy), "row", l, c)

            def modulation_back(l, what):
                act.wait_ge(sig("rows_stored"), 16 * 8 * (l + 1))
                for q, dst in what:
                    for c in range(2):
                        act.dma_start(dst[:, c], mod_dram[l, c, q * D:(q + 1) * D].partition_broadcast(128)).then_inc(sig("rows_back", q), 16)

            def tail(l):
                def rest(t):
                    act.wait_ge(sig("h2_ready"), NT * l + t + 1)
                    act.dma_start(h2_dram[t * 128:(t + 1) * 128, :], H2[t]).then_inc(sig("h2_stored"), 16)
                    p = take(act, "h2T", l, t)
                    if t >= 2:
                        act.wait_ge(sig("tile_routed"), (NT - 1) * l + t - 1)
                    took(act.activation(H2T[t % 2].rearrange("p k t -> p (k t)"), p[:, :], ACT.Copy), "h2T", l, t)

                if l == 0:
                    act.wait_ge(sig("outputs_stored"), 32)
                for t in range(NT):
                    act.wait_ge(sig("x_mixed"), 2 * NT * l + 2 * t + 2)
                    norm_tile(t, H2[t])
                    if t:
                        rest(t - 1)
                    if l == 0 and t >= 3:
                        shift_and_scale(1, [t - 1])
                rest(NT - 1)
                modulation_back(l, [(5, BC[:, 1])])
                act.wait_ge(sig("router_z"), 2 * l + 1)
                act.activation(scr(RT + 0, 20), scr(RT + 0, 20), ACT.Exp).then_inc(sig("router_exp"), 1)
                act.wait_ge(sig("router_z"), 2 * l + 2)
                act.activation(scr(RT + 20, 5), scr(RT + 20, 5), ACT.Exp).then_inc(sig("router_exp"), 1)

            def experts(l):
                xt, gu, hid, yd = (sig(n, l) for n in ("x_turned", "gate_up_done", "hidden", "down_done"))

                def turn(b1, par):
                    act.wait_ge(xt, b1)
                    act.activation(XGT[par].rearrange("p (b c) -> p b c", b=2), PB[A_][:, :].rearrange("p (b c) -> p b c", b=2)[:, :, 0:4 * CAP],
                                   ACT.Copy).then_inc(sig("x_ready", l), 1)

                def body(b, par, first, last, before):
                    for h in range(2):
                        act.wait_ge(gu, 2 * b + h + 1)
                        act.activation(SIL[:, 2 * CAP * h:2 * CAP * (h + 1)], PB[B_][:, 512 * h:512 * h + 2 * CAP],
                                       ACT.Silu).then_inc(sig("silu", l), 1)
                    if not last:
                        turn(b + 2, 1 - par)
                    act.wait_ge(yd, 2 * b + 1)
                    if before is not None:
                        act.wait_ge(sig("scattered", l, par), before)
                    act.activation(YR[par][0:CAP, 0:512], PB[C_][0:CAP, 0:512], ACT.Copy).then_inc(sig("y_left", l), 1)

                turn(1, 0)
                body(0, 0, True, False, None)
                body(1, 1, False, False, None)
                with nc.Fori(1, NE // 2 - 1, engines=(ACTE,)) as it:
                    for par in range(2):
                        body(2 * it + par, par, False, False, 16 * it)
                body(NE - 2, 0, False, False, 8 * NE - 16)
                body(NE - 1, 1, False, True, 8 * NE - 16)
                for i in range(2):
                    act.wait_ge(sig("scattered", l, i), 8 * NE)
                nb = act.value_load(NBK[0:1, 0:1], min_val=0, max_val=OVER)
                with act.If(nb > 0):
                    with nc.Fori(0, OVER, engines=(ACTE,)) as i:
                        with act.If(nb > i):
                            act.wait_ge(sig("more_turned", l), i + 1)
                            act.activation(XGT[0].rearrange("p (b c) -> p b c", b=2), PB[A_][:, :].rearrange("p (b c) -> p b c", b=2)[:, :, 0:4 * CAP],
                                           ACT.Copy).then_inc(sig("more_x_ready", l), 1)
                            act.wait_ge(sig("more_gate_up", l), i + 1)
                            act.activation(SIL.rearrange("p (h c) -> p h c", h=2), HALVES[:, :, 0:2 * CAP], ACT.Silu).then_inc(sig("more_silu", l), 1)
                            act.wait_ge(sig("more_down", l), i + 1)
                            act.activation(YR[0][0:CAP, 0:512], PB[C_][0:CAP, 0:512], ACT.Copy).then_inc(sig("more_left", l), 1)
                if l == 1:
                    act.dma_start(GF, a["g_final"].partition_broadcast(128)).then_inc(sig("final_gain"), 16)
                act.wait_ge(sig("row_weights"), l + 1)
                for t in range(NT):
                    act.wait_ge(sig("y_back", t), 16 * (l + 1))
                    act.activation(YB[t][:, 0:D], YB[t][:, 0:D], ACT.Copy, scale=WT1[:, t:t + 1]).then_inc(sig("y_first"), 1)

            def pooled_out(j):
                p = take(act, "pool", j)
                took(act.activation(CAT[:, j, :], p[:, 0:TOK], ACT.Copy, scale=pool_sT[:, j:j + 1]), "pool", j)

            first_norm(0)
            for j in range(HC):
                p = take(act, "ga", j)
                if j:
                    act.wait_ge(sig("u_ready"), j)
                took(act.activation(GA, p[:, 0:TOK], ACT.Copy), "ga", j)
                p = take(act, "gb", j)
                took(act.activation(SG, p[:, 0:TOK], ACT.Sigmoid), "gb", j)
                if j == 0:
                    tables_and_caches()
                if j == 1:
                    act.wait_ge(sig("lam_dots"), 1)
                    act.activation(laml, lam2, ACT.Exp).then_inc(sig("lam_exps"), 1)
                if j == 1:
                    modulation_row(0, 4, 0)
                    modulation_row(0, 5, 1)
            for name, dst in (("q", qT), ("k", kT)):
                for j in range(HC):
                    p = take(act, name, j)
                    took(act.activation(dst[:, j, :], p[:, 0:TOK], ACT.Copy), name, j)
            n = 0
            for name in VALUES_ORDER:
                if name[0] == "row":
                    modulation_row(0, name[2], name[2] - 4)
                    continue
                p = take(act, *name)
                if name[0] == "v":
                    took(act.activation(V[:, name[1], :], p[:, 0:HALF], ACT.Copy), *name)
                else:
                    if n:
                        act.wait_ge(sig("roped"), n)
                    n += 1
                    took(act.activation(RQ, p[:, 0:NS], ACT.Copy), *name)
            p = take(act, "mean")
            took(act.activation(MU[:, 0:TOK], p[:, 0:TOK], ACT.Copy, scale=1.0 / HALF), "mean")
            for j in range(HC):
                act.wait_ge(sig("centred"), j + 1)
                if j >= 2:
                    act.wait_ge(sig("squares_summed"), j - 1)
                act.activation(SQB[j % 2], UO[:, j, :], ACT.Square).then_inc(sig("conv_squares"), 1)
            p = take(act, "var")
            act.wait_ge(sig("eps_ready"), 1)
            act.wait_ge(sig("roped"), 8)
            took(act.activation(RS[:, 0:TOK], p[:, 0:TOK], ACT.Sqrt, bias=eps1, scale=1.0 / HALF), "var")
            modulation_row(0, 9, 5)
            p = take(act, "kcT")
            took(act.activation(kcT.rearrange("p h t -> p (h t)"), p[:, 0:HALF], ACT.Copy), "kcT")
            p = take(act, "kout")
            took(act.activation(KC, p[:, 0:HALF], ACT.Copy), "kout")
            after(act, "kout")
            act.dma_start(out["new_cache_k"].rearrange("b l t h c d -> (b l t) (h c d)"), KC).then_inc(sig("outputs_stored"), 16)
            after(act, "v", 4)
            act.dma_start(out["new_cache_v"].rearrange("b l t h c -> (b l t) (h c)"), V[:, 4, :]).then_inc(sig("outputs_stored"), 16)
            for j in range(HC):
                act.wait_ge(sig("conv_normed"), j + 1)
                act.activation(catU[:, j, 0:NS], UO[:, j, 0:NS], ACT.Silu, bias=ln_bT[:, j:j + 1], scale=ln_gT[:, j:j + 1])
                act.activation(catU[:, j, NS:], UO[:, j, 15 + NS:], ACT.Silu, bias=ln_bT[:, j:j + 1], scale=ln_gT[:, j:j + 1]).then_inc(sig("cat_u"), 1)
            modulation_row(0, 10, 6)
            def exps(u):
                w = NS + PAST if UNITS[u][0] < 4 else NP
                for c in range(2):
                    take(act, "s", u, c)
                    act.wait_ge(sig("max_ready"), 2 * u + c + 1)
                    if u >= 2 and c == 0:
                        take(act, "aT", u - 2)
                    took(act.activation(PR[:, u % 2, c, 0:w], PB[uses[("s", u, c)][0]][:, 0:w], ACT.Exp, bias=snb[:, u % 2, c:c + 1],
                                        scale=DH ** -0.5, accum_out=sl[:, u % 2, c:c + 1]), "s", u, c)

            def turned(u):
                w = NS + PAST if UNITS[u][0] < 4 else NP
                p = take(act, "aT", u)
                if u >= 2:
                    take(act, "av", u - 2)
                took(act.activation(AT[:, u % 2, 0:w], p[:, 0:w], ACT.Copy), "aT", u)

            NU = len(UNITS)
            for i in range(NU + 1):
                if i < NU:
                    exps(i)
                if i >= 1:
                    turned(i - 1)
                if i in SUMS_AT_UNIT:
                    kind, l, c = SUMS_AT_UNIT[i]
                    if kind == "row":
                        modulation_row(l, c, c - 4)
                    else:
                        shift_and_scale(l, [c])
                if i == 14:
                    modulation_back(0, [(2, BC[:, 0])])
            act.wait_ge(sig("o_mean_square"), 1)
            act.activation(orstd, orstd, ACT.Sqrt).then_inc(sig("o_root"), 1)
            act.wait_ge(sig("subln_ready"), 1)
            for h in range(HEADS):
                p = take(act, "oT", h)
                took(act.activation(oT[:, h, :], p[:, 0:TOK], ACT.Copy, scale=sub2), "oT", h)
            after(act, "oT", 3)
            modulation_back(0, [(4, M2[:, 0]), (3, M2[:, 1])])
            tail(0)
            experts(0)

            act.dma_start(PW, a["pool_w"][0].rearrange("g c e -> c g e")).then_inc(sig("pool_w_loaded"), 16)
            first_norm(1)
            for j in range(HC):
                p = take(act, "xc", j)
                if j:
                    act.wait_ge(sig("pooled"), j)
                else:
                    act.wait_ge(sig("pads_zero"), 1)
                act.activation(XP[:, 8:8 + NS], p[:, 0:NS], ACT.Copy)
                took(act.activation(XP[:, 16 + NS:16 + TOK], p[:, NS:TOK], ACT.Copy), "xc", j)
                if j:
                    pooled_out(j - 1)
                for c in SUMS_AT["xc"][j]:
                    modulation_row(1, c, 4 + c)
            for j in range(HC):
                p = take(act, "hd", j)
                if j:
                    act.wait_ge(sig("gated_in"), j)
                took(act.activation(HD, p[:, 0:TOK], ACT.Copy), "hd", j)
                p = take(act, "cg", j)
                took(act.activation(CG, p[:, 0:TOK], ACT.Copy), "cg", j)
                if j == 0:
                    pooled_out(HC - 1)
                for c in SUMS_AT["cg"][j]:
                    modulation_row(1, c, 4 + c)
            for j in range(HC):
                p = take(act, "bg", j)
                if j:
                    act.wait_ge(sig("short_conv"), j)
                took(act.activation(BG, p[:, 0:TOK], ACT.Copy), "bg", j)
                for c in SUMS_AT["bg"][j]:
                    modulation_row(1, c, 4 + c)
            modulation_back(1, [(2, BC[:, 0]), (4, M2[:, 0]), (3, M2[:, 1])])
            tail(1)
            experts(1)
            def store(t):
                act.wait_ge(sig("y_final"), t + 1)
                dst = out["y_sample"][0, 128 * t:128 * (t + 1), :] if t < 4 else out["y_prompt"][0]
                act.dma_start(dst, X[:, t, :]).then_inc(sig("outputs_stored"), 16)

            for t in range(NT):
                act.wait_ge(sig("combined", 1), t + 1)
                norm_tile(t, XN[:, t, :])
                if t:
                    store(t - 1)
            store(NT - 1)
            act.wait_ge(sig("outputs_stored"), 16 * (2 + NT))

        @block.vector
        def _(dve):
            link = chain(dve, "vector_step")
            tt, ts, stt = dve.tensor_tensor, dve.tensor_scalar, dve.scalar_tensor_tensor
            dve.memset(eps1, EPS).then_inc(sig("eps_ready"), 1)
            p = take(dve, "cond")
            took(dve.tensor_copy(condT[:, :], p[:, 0:16]), "cond")

            def row_products(l, c, chunks=range(DC)):
                n = ADA_NO[(l, c)]
                ini = INI[1 if (l, c // 4) == (1, 0) else 0][n % 2]
                s0, _ = page_at[("ada", l, c)]
                w = slot(s0).rearrange("p (k n) -> p k n", k=DC)
                if chunks[0] == 0:
                    page(dve, ("ada", l, c))
                    dve.wait_ge(sig("bias_row", n % 2), 16 * (n // 2 + 1))
                    if n == 0:
                        after(dve, "cond")
                    if n >= 2:
                        ll, cc = ADA_ORDER[n - 2]
                        take(dve, "adaT" if cc < 4 else "row", ll, cc)
                for k in chunks:
                    for s in range(2):
                        if k:
                            dve.wait_ge(sig("row_product"), ADA_OPS * n + 2 * k + s - 1)
                        stt(ACC[:, n % 2, s], w[:, k, :], condT[:, 8 * s + k:8 * s + k + 1], ACC[:, n % 2, s] if k else ini,
                            ALU.mult, ALU.add).then_inc(sig("row_product"), 1)

            def scale1(l):
                for c in range(4):
                    after(dve, "adaT", l, c)
                stt(SC1[:, l], MOD[:, l, 8:16, :], 1.0, g_n1T[:, l, :].unsqueeze(2).broadcast_to([128, DC, 2]),
                    ALU.add, ALU.mult).then_inc(sig("modulated", l), 1)

            NORM = [0]

            def inverse_root(t):
                NORM[0] += 1
                dve.wait_ge(sig("squares_done"), NORM[0])
                ts(rstd[:, t:t + 1], ssq[:, t:t + 1], 1.0 / D, EPS, ALU.mult, ALU.add).then_inc(sig("mean_square"), 1)
                dve.wait_ge(sig("root_done"), NORM[0])
                link(dve.reciprocal(rstd[:, t:t + 1], rstd[:, t:t + 1]))

            def normed(l):
                for t in range(NT):
                    inverse_root(t)
                    ts(XN[:, t, :], X[:, t, :], rstd[:, t:t + 1], None, ALU.mult).then_inc(sig("normed", l), 1)

            def modulated(l):
                for k in range(1, DC, 2):
                    if k == 1:
                        dve.wait_ge(sig("modulated", l), 1)
                    p = take(dve, "hT", l, k)
                    ts(hT[:, k, 0:NS], p[:, 0:NS], SC1[:, l, k, 0:1], MOD[:, l, k, 0:1], ALU.mult, ALU.add)
                    took(ts(hT[:, k, NS:], p[:, NS:TOK], SC1[:, l, k, 1:2], MOD[:, l, k, 1:2], ALU.mult, ALU.add), "hT", l, k)

            def tail(l):
                dve.wait_ge(sig("rows_back", 2), 32 * (l + 1))
                for t in range(NT):
                    for n in range(2):
                        p = take(dve, "out", l, t, n)
                        cols = slice(n * 512, (n + 1) * 512)
                        took(tt(TMP, p[:, 0:512], BC[:, 0, cond_of(t), cols], ALU.mult), "out", l, t, n)
                        after(dve, "out", l, t, n)
                        tt(X[:, t, cols], X[:, t, cols], TMP, ALU.add).then_inc(sig("x_mixed"), 1)
                        dve.wait_ge(sig("x_mixed"), 2 * NT * l + 2 * t + n + 1)
                    inverse_root(t)
                    if t == 0:
                        dve.wait_ge(sig("rows_back", 4), 32 * (l + 1))
                        dve.wait_ge(sig("rows_back", 3), 32 * (l + 1))
                    link(stt(H2[t], X[:, t, :], rstd[:, t:t + 1], M2[:, 0, cond_of(t)], ALU.mult, ALU.mult))
                    tt(H2[t], H2[t], M2[:, 1, cond_of(t)], ALU.add).then_inc(sig("h2_ready"), 1)
                    if l == 0 and t < 4:
                        row_products(1, 2 + t // 2, range(4 * (t % 2), 4 * (t % 2) + 4))

            def routing(l):
                at = [RT + 25]
                dve.wait_ge(sig("tables_loaded"), 16 * 17)

                def tmp(*shape):
                    n = int(np.prod(shape))
                    v = scr(at[0], n)
                    at[0] += n
                    if len(shape) == 2:
                        v = v.rearrange("p (a b) -> p a b", a=shape[0])
                    if len(shape) == 3:
                        v = v.rearrange("p (a b c) -> p a b c", a=shape[0], b=shape[1])
                    return v

                LG = tmp(NT, 36)
                if l == 0:
                    scale1(1)
                p = take(dve, "logit", l)
                took(tt(LG, p[:, 512:512 + 36 * NT].rearrange("p (t n) -> p t n", t=NT), BR[:, l, :].unsqueeze(1).broadcast_to([128, NT, 36]), ALU.add), "logit", l)
                after(dve, "logit", l)
                gl = LG[:, :, 0:NG]
                el = LG[:, :, NG:].rearrange("p t (g e) -> p t g e", g=NG)
                top = lambda v, n: v.unsqueeze(2).broadcast_to([128, NT, n])
                gm, gi = tmp(NT), tmp(NT)
                oh = tmp(NT, NG)
                z = scr(RT, 20).rearrange("p (t g) -> p t g", g=NG)
                iog = iota["g"].unsqueeze(1).broadcast_to([128, NT, NG])
                ioe = iota["e"].unsqueeze(1).broadcast_to([128, NT, EPG])
                link(dve.tensor_reduce(gm, gl, AX_X, ALU.max))
                tt(z, gl, top(gm, NG), ALU.subtract).then_inc(sig("router_z"), 1)
                link(tt(oh, gl, top(gm, NG), ALU.is_equal))
                link(tt(oh, oh, iog, ALU.mult))
                link(dve.tensor_reduce(gi, oh, AX_X, ALU.min))
                link(tt(oh, iog, top(gi, NG), ALU.is_equal))
                prod, e8 = tmp(NT * NG, EPG), tmp(NT, EPG)
                pv = prod.rearrange("p (t g) e -> p t g e", g=NG)
                link(tt(pv, el, oh.unsqueeze(3).broadcast_to([128, NT, NG, EPG]), ALU.mult))
                link(dve.tensor_reduce(e8, pv.rearrange("p t g e -> p t e g"), AX_X, ALU.add))
                ohe = tmp(2, NT * EPG).rearrange("p k (t e) -> p k t e", t=NT)
                vm, vi = tmp(2, NT), tmp(NT)
                for k in range(2):
                    link(dve.tensor_reduce(vm[:, k], e8, AX_X, ALU.max))
                    link(tt(ohe[:, k], e8, top(vm[:, k], EPG), ALU.is_equal))
                    link(tt(ohe[:, k], ohe[:, k], ioe, ALU.mult))
                    link(dve.tensor_reduce(vi, ohe[:, k], AX_X, ALU.min))
                    link(tt(ohe[:, k], ioe, top(vi, EPG), ALU.is_equal))
                    if k == 0:
                        link(stt(e8, ohe[:, 0], -3e38, e8, ALU.mult, ALU.add))
                e2 = scr(RT + 20, 5)
                tt(e2, vm[:, 1], vm[:, 0], ALU.subtract).then_inc(sig("router_z"), 1)
                ch, pairs = tmp(2, NT * NE), tmp(2, NT * NE)
                ch5 = ch.rearrange("p k (t g e) -> p k t g e", t=NT, g=NG)
                for k in range(2):
                    for t in range(NT):
                        ins = tt(ch5[:, k, t], oh[:, t, :].unsqueeze(2).broadcast_to([128, NG, EPG]),
                                 ohe[:, k, t, :].unsqueeze(1).broadcast_to([128, NG, EPG]), ALU.mult)
                link(ins)
                tt(CHB[:, :], ch[:, 0], ch[:, 1], ALU.add).then_inc(sig("chosen"), 1)
                p = take(dve, "rank", l)
                rk = tmp(192)
                took(dve.tensor_copy(rk, p[:, 0:192]), "rank", l)
                after(dve, "rank", l)
                ranks, cnt = rk[:, 0:160], rk[:, 160:192]
                nov, ove, start, one = tmp(NE), tmp(NE), tmp(NE), tmp(NE)
                cmp = tmp(NE * (MORE + 1))
                c3 = cmp[:, 0:NE * MORE].rearrange("p (a b) -> p a b", a=NE)
                dve.memset(one, 1.0)
                link(tt(c3, cnt.unsqueeze(2).broadcast_to([128, NE, MORE]), iota["m"].unsqueeze(1).broadcast_to([128, NE, MORE]), ALU.is_gt))
                link(dve.tensor_reduce(nov, c3, AX_X, ALU.add))
                link(dve.tensor_tensor_scan(ove, one, nov, 0.0, ALU.mult, ALU.add))
                link(tt(start, ove, nov, ALU.subtract))
                res = tmp(3, 2 * NT)
                for w in range(3):
                    for k in range(2):
                        c3 = pairs[:, k].rearrange("p (t e) -> p t e", t=NT)
                        m1 = ch[:, k].rearrange("p (t e) -> p t e", t=NT)
                        m2 = (ranks.rearrange("p (t e) -> p t e", t=NT), iota["E"].unsqueeze(1).broadcast_to([128, NT, NE]),
                              start.unsqueeze(1).broadcast_to([128, NT, NE]))[w]
                        ins = tt(c3, m1, m2, ALU.mult)
                    link(ins)
                    link(dve.tensor_reduce(res[:, w], pairs.rearrange("p k (t e) -> p (k t) e", t=NT), AX_X, ALU.add))
                rank, exp_, st_ = res[:, 0], res[:, 1], res[:, 2]
                q, gt = tmp(10), tmp(10)
                c3 = cmp[:, 0:10 * MORE].rearrange("p (a b) -> p a b", a=10)
                link(tt(c3, rank.unsqueeze(2).broadcast_to([128, 10, MORE]), iota["m"].unsqueeze(1).broadcast_to([128, 10, MORE]), ALU.is_ge))
                ts(gt, rank, float(CAP), None, ALU.is_ge)
                link(dve.tensor_reduce(q, c3, AX_X, ALU.add))
                tt(st_, st_, q, ALU.add)
                link(stt(rank, q, -float(CAP), rank, ALU.mult, ALU.add))
                link(stt(st_, st_, float(NE - 1), exp_, ALU.add, ALU.subtract))
                link(tt(st_, st_, gt, ALU.mult))
                link(tt(exp_, exp_, st_, ALU.add))
                tt(POSH, iota["c"].unsqueeze(1).broadcast_to([128, 10, CAP]), rank.unsqueeze(2).broadcast_to([128, 10, CAP]), ALU.is_equal)
                link(tt(EQB, iota["b"].unsqueeze(1).broadcast_to([128, 10, NBLK]), exp_.unsqueeze(2).broadcast_to([128, 10, NBLK]), ALU.is_equal))
                for s in range(2):
                    ins = tt(VAL[:, s], EQB, ROWS[:, s].rearrange("p k t -> p (k t)").unsqueeze(2).broadcast_to([128, 10, NBLK]), ALU.mult)
                ins.then_inc(sig("one_hots"), 1)
                ebk = tmp(OVER)
                for lo in range(0, OVER, MORE + 1):
                    m = min(MORE + 1, OVER - lo)
                    c3 = cmp[:, 0:m * NE].rearrange("p (a b) -> p a b", a=m)
                    link(tt(c3, ove.unsqueeze(1).broadcast_to([128, m, NE]),
                            iota["o"][:, lo:lo + m].unsqueeze(2).broadcast_to([128, m, NE]), ALU.is_le))
                    link(dve.tensor_reduce(ebk[:, lo:lo + m], c3, AX_X, ALU.add))
                link(ts(ebk, ebk, float(NE - 1), None, ALU.min))
                dve.tensor_copy(NBK[:, 0:1], ove[:, NE - 1:NE])
                link(dve.tensor_copy(NBK[:, 1:], ebk))
                p = take(dve, "table", l)
                took(ts(IDX[0:CAP, :], p[0:CAP, 0:2 * NBLK], NOROW, None, ALU.add), "table", l)
                after(dve, "table", l)
                dve.memset(small[:, 157:158], 0.0).then_inc(sig("routed"), 1)
                dve.wait_ge(sig("router_exp"), 2 * l + 1)
                gs = tmp(NT)
                link(dve.tensor_reduce(gs, z, AX_X, ALU.add))
                dve.wait_ge(sig("router_exp"), 2 * l + 2)
                d2 = tmp(NT)
                link(ts(d2, e2, 1.0, None, ALU.add))
                link(tt(gs, gs, d2, ALU.mult))
                link(dve.reciprocal(WT1, gs))
                tt(WT2, WT1, e2, ALU.mult).then_inc(sig("row_weights"), 1)

            def experts(l):
                def body(b, par, before):
                    for h in range(2):
                        dve.wait_ge(sig("silu", l), 2 * b + h + 1)
                        cols = slice(2 * CAP * h, 2 * CAP * (h + 1))
                        tt(HIDT[par][:, cols], PB[B_][:, 512 * h + 2 * CAP:512 * h + 4 * CAP], SIL[:, cols], ALU.mult).then_inc(sig("hidden", l), 1)
                    dve.wait_ge(sig("down_done", l), 2 * b + 2)
                    if before is not None:
                        dve.wait_ge(sig("scattered", l, par), before)
                    dve.tensor_copy(YR[par][0:CAP, 512:1024], PB[C_][0:CAP, 512:1024]).then_inc(sig("y_right", l), 1)

                body(0, 0, None)
                body(1, 1, None)
                with nc.Fori(1, NE // 2, engines=(DVE,)) as it:
                    for par in range(2):
                        body(2 * it + par, par, 16 * it)
                for i in range(2):
                    dve.wait_ge(sig("scattered", l, i), 8 * NE)
                nb = dve.value_load(NBK[0:1, 0:1], min_val=0, max_val=OVER)
                with dve.If(nb > 0):
                    with nc.Fori(0, OVER, engines=(DVE,)) as i:
                        with dve.If(nb > i):
                            dve.wait_ge(sig("more_silu", l), i + 1)
                            tt(HIDT[0].rearrange("p (h c) -> p h c", h=2), HALVES[:, :, 2 * CAP:4 * CAP], SIL.rearrange("p (h c) -> p h c", h=2),
                               ALU.mult).then_inc(sig("more_hidden", l), 1)
                            dve.wait_ge(sig("more_down", l), i + 1)
                            dve.tensor_copy(YR[0][0:CAP, 512:1024], PB[C_][0:CAP, 512:1024]).then_inc(sig("more_right", l), 1)
                dve.wait_ge(sig("rows_back", 5), 32 * (l + 1))
                for t in range(NT):
                    dve.wait_ge(sig("y_first"), NT * l + t + 1)
                    y = YB[t]
                    link(stt(y[:, 0:D], y[:, D:], WT2[:, t:t + 1], y[:, 0:D], ALU.mult, ALU.add))
                    tt(y[:, 0:D], y[:, 0:D], BC[:, 1, cond_of(t)], ALU.mult).then_inc(sig("y_gated"), 1)

            row_products(0, 0)
            normed(0)
            row_products(0, 2)
            for i, (dst, w) in enumerate(((P1, 32), (P2, 125), (P3, 12))):
                p = take(dve, "par", i + 1)
                took(dve.tensor_copy(dst[:, :], p[:, 0:w]), "par", i + 1)
            for i in (1, 2, 3):
                after(dve, "par", i)
            ts(sub2, sublnT, 1.0 - LAM_INIT, None, ALU.mult).then_inc(sig("subln_ready"), 1)

            link(dve.tensor_copy(strict_bf[:, :], strict))
            dve.memset(ones_bf[:, :], 1.0).then_inc(sig("bf_ready"), 1)

            scale1(0)
            modulated(0)
            dve.wait_ge(sig("lam_loaded"), 64)
            lv = LAMV.rearrange("p (i two d) -> p i two d", i=2, two=2)
            link(tt(lv[:, :, 0, :], lv[:, :, 0, :], lv[:, :, 1, :], ALU.mult))
            dve.tensor_reduce(lam2, lv[:, :, 0, :], AX_X, ALU.add).then_inc(sig("lam_dots"), 1)
            row_products(0, 4)
            row_products(0, 5)
            for j in range(HC):
                dve.wait_ge(sig("u_ready"), j + 1)
                ts(UO[:, j, :], UP[:, j, 0:UOW], conv_wT[:, 0, j:j + 1], conv_bT[:, j:j + 1], ALU.mult, ALU.add).then_inc(sig("conv_step", j), 1)
                for tap in range(1, TAPS):
                    dve.wait_ge(sig("conv_step", j), tap)
                    stt(UO[:, j, :], UP[:, j, tap:tap + UOW], conv_wT[:, tap, j:j + 1], UO[:, j, :], ALU.mult, ALU.add).then_inc(sig("conv_step", j), 1)
            for c in range(6, 10):
                row_products(0, c)
            row_products(0, 10)
            dve.wait_ge(sig("lam_exps"), 1)
            link(tt(lam_neg, laml[:, 1:2], laml[:, 0:1], ALU.subtract))
            link(ts(lam_neg, lam_neg, -LAM_INIT, None, ALU.add))
            after(dve, "mean")
            for j in range(HC):
                dve.wait_ge(sig("conv_step", j), TAPS)
                tt(UO[:, j, 0:NS], UO[:, j, 0:NS], MU[:, 0:NS], ALU.subtract)
                tt(UO[:, j, 15 + NS:], UO[:, j, 15 + NS:], MU[:, NS:TOK], ALU.subtract).then_inc(sig("centred"), 1)
            after(dve, "var")
            link(dve.reciprocal(RS[:, 0:TOK], RS[:, 0:TOK]))
            dve.wait_ge(sig("centred"), HC)
            dve.wait_ge(sig("conv_squares"), HC)
            for j in range(HC):
                tt(UO[:, j, 0:NS], UO[:, j, 0:NS], RS[:, 0:NS], ALU.mult)
                tt(UO[:, j, 15 + NS:], UO[:, j, 15 + NS:], RS[:, NS:TOK], ALU.mult).then_inc(sig("conv_normed"), 1)

            def maxima(u):
                w = NS + PAST if UNITS[u][0] < 4 else NP
                for c in range(2):
                    p = take(dve, "s", u, c)
                    link(dve.tensor_reduce(smx[:, u % 2, c:c + 1], p[:, 0:w], AX_X, ALU.max))
                    ts(snb[:, u % 2, c:c + 1], smx[:, u % 2, c:c + 1], -DH ** -0.5, None, ALU.mult).then_inc(sig("max_ready"), 1)

            def mixed(u):
                w = NS + PAST if UNITS[u][0] < 4 else NP
                for c in range(2):
                    after(dve, "s", u, c)
                link(dve.reciprocal(sr[:, u % 2, :], sl[:, u % 2, :]))
                link(tt(sr[:, u % 2, 1:2], sr[:, u % 2, 1:2], lam_neg, ALU.mult))
                link(ts(PR[:, u % 2, 1, 0:w], PR[:, u % 2, 1, 0:w], sr[:, u % 2, 1:2], None, ALU.mult))
                stt(PR[:, u % 2, 0, 0:w], PR[:, u % 2, 0, 0:w], sr[:, u % 2, 0:1], PR[:, u % 2, 1, 0:w], ALU.mult, ALU.add).then_inc(sig("a_ready"), 1)

            def heads_out(u):
                t, h = UNITS[u]
                p = take(dve, "av", u)
                took(dve.tensor_copy(OR[:, t, h * 128:(h + 1) * 128], p[:, 0:128]), "av", u)

            NU = len(UNITS)
            for i in range(NU + 2):
                if 1 <= i <= NU:
                    mixed(i - 1)
                if i < NU:
                    maxima(i)
                if i < 2:
                    row_products(0, 11, range(4 * i, 4 * i + 4))
                if 2 <= i < 18:
                    page_no, eighth = divmod(i - 2, 8)
                    row_products(1, page_no, range(eighth, eighth + 1))
                if i >= 2:
                    heads_out(i - 2)
            after(dve, "av", NU - 1)
            sq = PR.rearrange("p u c t -> p (u c t)")
            flat = OR.rearrange("p t n -> p (t n)")
            link(tt(sq, flat, flat, ALU.mult))
            link(dve.tensor_reduce(oss, sq.rearrange("p (u e) -> p u e", e=128), AX_X, ALU.add))
            ts(orstd, oss, 1.0 / 128, EPS, ALU.mult, ALU.add).then_inc(sig("o_mean_square"), 1)
            dve.wait_ge(sig("o_root"), 1)
            link(dve.reciprocal(orstd, orstd))
            o3 = flat.rearrange("p (u e) -> p u e", e=128)
            tt(o3, o3, orstd.unsqueeze(2).broadcast_to([128, 20, 128]), ALU.mult).then_inc(sig("o_normed"), 1)
            tail(0)
            routing(0)
            experts(0)

            normed(1)
            modulated(1)
            dve.wait_ge(sig("pads_zero"), 1)
            for j in range(HC):
                after(dve, "xc", j)
                src, n = XP, XPW
                for s in range(j + 1):
                    n -= 1 << s
                    dst = PS2[s % 2]
                    link(tt(dst[:, 0:n], src[:, 0:n], src[:, 1 << s:(1 << s) + n], ALU.add))
                    src = dst
                half = WINDOWS[j] // 2
                for at, m in ((8 - half, NS), (16 + NS - half, NP)):
                    for e, lo in ((0, at), (1, at + m - 8)):
                        ins = tt(src[:, lo:lo + 8], src[:, lo:lo + 8], EDG[:, j, e], ALU.mult)
                link(ins)
                if j >= 2:
                    take(dve, "pool", j - 2)
                stt(DP[:, j % 2, 0:NS], src[:, 8 - half:8 - half + NS], 1.0 / WINDOWS[j], XP[:, 8:8 + NS], ALU.mult, ALU.subtract)
                stt(DP[:, j % 2, NS:], src[:, 16 + NS - half:16 + TOK - half], 1.0 / WINDOWS[j], XP[:, 16 + NS:16 + TOK],
                    ALU.mult, ALU.subtract).then_inc(sig("pooled"), 1)
                for c in PRODUCTS_AT["xc"][j]:
                    row_products(1, c)
            for j in range(HC):
                after(dve, "cg", j)
                after(dve, "hd", j)
                tt(TP[:, j, 1:1 + NS], HD[:, 0:NS], CG[:, 0:NS], ALU.mult)
                tt(TP[:, j, 2 + NS:2 + TOK], HD[:, NS:], CG[:, NS:], ALU.mult).then_inc(sig("gated_in"), 1)
                for c in PRODUCTS_AT["cg"][j]:
                    row_products(1, c)
            for j in range(HC):
                W3 = TOK + 1
                dve.wait_ge(sig("gated_in"), j + 1)
                if j:
                    dve.wait_ge(sig("short_conv"), j)
                link(ts(CA[:, 0:W3], TP[:, j, 0:W3], sconv_wT[:, 0, j:j + 1], None, ALU.mult))
                link(stt(CA[:, 0:W3], TP[:, j, 1:1 + W3], sconv_wT[:, 1, j:j + 1], CA[:, 0:W3], ALU.mult, ALU.add))
                link(stt(CA[:, 0:W3], TP[:, j, 2:2 + W3], sconv_wT[:, 2, j:j + 1], CA[:, 0:W3], ALU.mult, ALU.add))
                after(dve, "bg", j)
                tt(CAT[:, 4 + j, 0:NS], CA[:, 0:NS], BG[:, 0:NS], ALU.mult)
                tt(CAT[:, 4 + j, NS:], CA[:, 1 + NS:1 + TOK], BG[:, NS:], ALU.mult).then_inc(sig("short_conv"), 1)
                for c in PRODUCTS_AT["bg"][j]:
                    row_products(1, c)
            tail(1)
            routing(1)
            experts(1)
            dve.wait_ge(sig("final_gain"), 16)
            for t in range(NT):
                inverse_root(t)
                stt(X[:, t, :], X[:, t, :], rstd[:, t:t + 1], GF, ALU.mult, ALU.mult).then_inc(sig("y_final"), 1)

        @block.tensor
        def _(pe):
            mm = pe.matmul
            rows4, rows1, rows2, rows3 = (scr(14336 + 128 * i, 128) for i in range(4))
            pe.wait_ge(sig("consts_loaded"), 16)
            p = fill(pe, "cond")
            pe.wait_ge(sig("cond_ready"), 1)
            filled(pe.transpose(p[:, 0:16], rows4[0:16, :], ident[0:16, 0:16]), "cond")

            def turned_sums(l, c):
                n = ADA_NO[(l, c)]
                p = fill(pe, "adaT", l, c)
                pe.wait_ge(sig("row_product"), ADA_OPS * (n + 1))
                for m in range(4):
                    for s in range(2):
                        ins = mm(p[:, 2 * m + s:2 * m + s + 1], ACC[:, n % 2, s, m * 128:(m + 1) * 128], ones[:, 0:1], start=True, stop=True)
                filled(ins, "adaT", l, c)

            def row_sums(l, c):
                n = ADA_NO[(l, c)]
                p = fill(pe, "row", l, c)
                pe.wait_ge(sig("row_product"), ADA_OPS * (n + 1))
                for s in range(2):
                    ins = mm(p[0:2, 0:512], SEL[s], ACC[:, n % 2, s], start=(s == 0), stop=(s == 1))
                filled(ins, "row", l, c)

            def first_norm(l):
                pe.wait_ge(sig("normed", l), NT)
                for k in range(DC):
                    p = fill(pe, "hT", l, k)
                    for t in range(NT):
                        ins = pe.transpose(p[:, t * 128:(t + 1) * 128], XN[:, t, k * 128:(k + 1) * 128], ident)
                    filled(ins, "hT", l, k)
                for k in (DC - 2, DC - 1):
                    after(pe, "hT", l, k)

            def project(w, j, *name):
                p = fill(pe, *name)
                for cols in (slice(0, NS), slice(NS, TOK)):
                    for k in range(DC):
                        ins = mm(p[:, cols], w[:, k, j * 128:(j + 1) * 128], hT[:, k, cols], start=(k == 0), stop=(k == DC - 1))
                filled(ins, *name)
                return ins

            def page_used(n=1):
                pe.drain().then_inc(sig("mixer_page_used"), n)

            def tail(l, tag, cat):
                if l == 0:
                    pe.wait_ge(sig("tables_loaded"), 16 * 17)

                def logits(t):
                    pe.wait_ge(sig("h2_ready"), NT * l + t + 1)
                    p = fill(pe, "h2T", l, t)
                    for k in range(DC):
                        ins = pe.transpose(p[:, k * 128:(k + 1) * 128], H2[t][:, k:D:DC], ident)
                    filled(ins, "h2T", l, t)

                def router_product(t):
                    lg = PB[D_][:, 512:512 + 36 * NT]
                    after(pe, "h2T", l, t)
                    for k in range(DC):
                        ins = mm(lg[:, 36 * t:36 * t + 36], H2T[t % 2][:, k, :], WR[:, l, k, :], start=(k == 0), stop=(k == DC - 1))
                    if t < NT - 1:
                        ins.then_inc(sig("tile_routed"), 1)
                    return ins

                w = [page(pe, (tag, n)) for n in range(2)]
                for t in range(NT):
                    for n in range(2):
                        p = fill(pe, "out", l, t, n)
                        for k in range(DC):
                            ins = mm(p[:, 0:512], cat(k)[:, t * 128:(t + 1) * 128], w[n][:, k, :], start=(k == 0), stop=(k == DC - 1))
                        filled(ins, "out", l, t, n)
                    if t == NT - 1:
                        page_used(2)
                        pe.sem_inc(sig("mixer_out_done"), 1)
                    if t:
                        logits(t - 1)
                    if t >= 2:
                        router_product(t - 2)
                    if l == 0 and t >= 3:
                        turned_sums(1, t - 1)
                router_product(NT - 2)
                logits(NT - 1)
                fill(pe, "logit", l)
                filled(router_product(NT - 1), "logit", l)

            def ranks_and_table(l):
                pe.wait_ge(sig("bf_ready"), 1)
                pe.wait_ge(sig("chosen"), l + 1)
                p = fill(pe, "rank", l)
                for t in range(NT):
                    for s in range(t + 1):
                        mm(p[:, NE * t:NE * (t + 1)], strict_bf[:, :] if s == t else ones_bf[:, :], CHB[:, NE * s:NE * (s + 1)], start=(s == 0), stop=(s == t))
                for t in range(NT):
                    ins = mm(p[:, 160:192], ones_bf[:, :], CHB[:, NE * t:NE * (t + 1)], start=(t == 0), stop=(t == NT - 1))
                filled(ins, "rank", l)
                pe.wait_ge(sig("one_hots"), l + 1)
                p = fill(pe, "table", l)
                for i in range(10):
                    ins = mm(p[0:CAP, 0:2 * NBLK], POSH[:, i, :], VAL[:, :, i, :], start=(i == 0), stop=(i == 9))
                filled(ins, "table", l)

            def experts(l):
                fulls = moe_base[l][0]

                def turn_rows(par, ins_sem):
                    for k in range(DC):
                        at = (k // 4) * 512 + (k % 4) * CAP
                        ins = pe.transpose(PB[A_][:, at:at + CAP], XG[par][0:CAP, k:D:DC], ident[0:CAP, 0:CAP])
                    ins.then_inc(ins_sem, 1)

                def gate_up(s0, par, half):
                    wg, wu = (slot(s0 + i).rearrange("p (k n) -> p k n", k=DC) for i in range(2))
                    for j in (2 * half, 2 * half + 1):
                        for i, w in enumerate((wg, wu)):
                            at = 512 * half + (2 * i + j % 2) * CAP
                            for k in range(DC):
                                ins = mm(PB[B_][:, at:at + CAP], w[:, k, j * 128:(j + 1) * 128],
                                         XGT[par][:, k * CAP:(k + 1) * CAP], start=(k == 0), stop=(k == DC - 1))
                    return ins

                def down(s0, par, n, gate=None):
                    wd = slot(s0 + 2).rearrange("p (j n) -> p j n", j=HC)
                    for j in range(HC):
                        if j == 2 and gate is not None:
                            gate()
                        ins = mm(PB[C_][0:CAP, n * 512:(n + 1) * 512], HIDT[par][:, j * CAP:(j + 1) * CAP], wd[:, j, n * 512:(n + 1) * 512],
                                 start=(j == 0), stop=(j == HC - 1))
                    return ins

                def body(b, par, fill_no, first, last, gath):
                    s0 = 3 * par
                    for kind in range(2):
                        pe.wait_ge(slot_full[s0 + kind], fill_no(s0 + kind))
                    pe.wait_ge(sig("x_ready", l), b + 1)
                    if not first:
                        pe.wait_ge(sig("hidden", l), 2 * b)
                    for half in range(2):
                        gate_up(s0, par, half).then_inc(sig("gate_up_done", l), 1)
                    if not last:
                        pe.wait_ge(sig("gathered", l, 1 - par), gath)
                        turn_rows(1 - par, sig("x_turned", l))
                    pe.wait_ge(slot_full[s0 + 2], fill_no(s0 + 2))
                    pe.wait_ge(sig("hidden", l), 2 * b + 1)
                    if not first:
                        pe.wait_ge(sig("y_left", l), b)
                        pe.wait_ge(sig("y_right", l), b)
                    down(s0, par, 0, lambda: pe.wait_ge(sig("hidden", l), 2 * b + 2)).then_inc(sig("down_done", l), 1)
                    down(s0, par, 1).then_inc(sig("down_done", l), 1)

                pe.wait_ge(sig("gathered", l, 0), 16)
                turn_rows(0, sig("x_turned", l))
                body(0, 0, lambda s: 16 * (fulls[s] + 1), True, False, 16)
                body(1, 1, lambda s: 16 * (fulls[s] + 1), False, False, 32)
                with nc.Fori(1, NE // 2 - 1, engines=(PE,)) as it:
                    for par in range(2):
                        body(2 * it + par, par, lambda s: 16 * it + 16 * (fulls[s] + 1), False, False, 16 * it + 16 + 16 * par)
                body(NE - 2, 0, lambda s: 16 * (fulls[s] + NE // 2), False, False, 8 * NE)
                body(NE - 1, 1, lambda s: 16 * (fulls[s] + NE // 2), False, True, None)
                pe.wait_ge(sig("y_left", l), NE)
                pe.wait_ge(sig("y_right", l), NE)
                nb = pe.value_load(NBK[0:1, 0:1], min_val=0, max_val=OVER)
                with pe.If(nb > 0):
                    with nc.Fori(0, OVER, engines=(PE,)) as i:
                        with pe.If(nb > i):
                            pe.wait_ge(sig("more_gathered", l), 16 * i + 16)
                            turn_rows(0, sig("more_turned", l))
                            pe.wait_ge(sig("more_x_ready", l), i + 1)
                            pe.wait_ge(sig("more_weights", l), 48 * i + 48)
                            gate_up(0, 0, 0)
                            gate_up(0, 0, 1).then_inc(sig("more_gate_up", l), 1)
                            pe.wait_ge(sig("more_hidden", l), i + 1)
                            down(0, 0, 0)
                            down(0, 0, 1).then_inc(sig("more_down", l), 1)

            def feature_parameters():
                pe.wait_ge(sig("params_loaded"), 16 * 8)
                for n, (src, w) in enumerate(((rows1, 32), (rows2, 125), (rows3, 12))):
                    p = fill(pe, "par", n + 1)
                    filled(pe.transpose(p[:, 0:w], src[0:w, :], ident[0:w, 0:w]), "par", n + 1)

            for i, c in enumerate(ON_PE):
                w = page(pe, ("ada", 0, c))
                p = fill(pe, "row", 0, c)
                after(pe, "cond")
                for k in range(DC):
                    mm(p[0:2, 0:512], condT[:, k:16:8], w[:, k, :], start=(k == 0), stop=False)
                pe.wait_ge(sig("bias_for_pe", i), 16)
                filled(mm(p[0:2, 0:512], ones[:, 0:2], PE_BIAS[i], start=False, stop=True), "row", 0, c)
                pe.drain().then_inc(sig("ada_page_used"), 1)
                turned_sums(0, c - 1)
                after(pe, "row", 0, c)
                p = fill(pe, "adaT", 0, c)
                for m in range(4):
                    ins = mm(p[:, 2 * m:2 * m + 2], MALL[:, m * 128:(m + 1) * 128], ident[:, 0:2], start=True, stop=True)
                filled(ins, "adaT", 0, c)
                if i == 0:
                    feature_parameters()
            first_norm(0)
            wa, wb = page(pe, ("in_e", 0)), page(pe, ("in_e", 1))
            for j in range(HC):
                project(wa, j, "ga", j)
                project(wb, j, "gb", j)
                if j == 1:
                    row_sums(0, 4)
                    row_sums(0, 5)
            page_used(2)
            for c, name in ((2, "q"), (3, "k")):
                w = page(pe, ("in_e", c))
                for j in range(HC):
                    project(w, j, name, j)
                page_used()
            w = page(pe, ("in_e", 4))
            for name in VALUES_ORDER:
                if name[0] == "row":
                    row_sums(*name[1:])
                elif name[0] == "v":
                    p = fill(pe, *name)
                    for k in range(DC):
                        ins = mm(p[:, 0:HALF], hT[:, k, name[1] * 128:(name[1] + 1) * 128], w[:, k, :], start=(k == 0), stop=(k == DC - 1))
                    filled(ins, *name)
                else:
                    after(pe, *name[1:])
                    p = fill(pe, *name)
                    filled(mm(p[:, 0:NS], rot, {"q": qT, "k": kT}[name[1]][:, name[2], 0:NS], start=True, stop=True), *name)
            page_used()
            p = fill(pe, "mean")
            for cols, src in ((slice(0, NS), slice(0, NS)), (slice(NS, TOK), slice(15 + NS, 15 + TOK))):
                for j in range(HC):
                    pe.wait_ge(sig("conv_step", j), TAPS)
                    ins = mm(p[:, cols], ones, UO[:, j, src], start=(j == 0), stop=(j == HC - 1))
            filled(ins, "mean")
            p = fill(pe, "var")
            for j in range(HC):
                pe.wait_ge(sig("conv_squares"), j + 1)
                mm(p[:, 0:NS], ones, SQB[j % 2][:, 0:NS], start=(j == 0), stop=(j == HC - 1))
                ins = mm(p[:, NS:TOK], ones, SQB[j % 2][:, 15 + NS:15 + TOK], start=(j == 0), stop=(j == HC - 1))
                if j < HC - 1:
                    ins.then_inc(sig("squares_summed"), 1)
            filled(ins, "var")
            row_sums(0, 9)
            pe.wait_ge(sig("cache_loaded"), 32)
            p = fill(pe, "kcT")
            for h in range(HEADS):
                ins = pe.transpose(p[:, h * 128:(h + 1) * 128], KC[:, h * 128:(h + 1) * 128], ident)
            filled(ins, "kcT")
            p = fill(pe, "kout")
            for h in range(HEADS):
                ins = pe.transpose(p[:, h * 128:(h + 1) * 128], kT[:, h, NS:], ident)
            filled(ins, "kout")
            row_sums(0, 10)
            def scores(u):
                t, h = UNITS[u]
                for c in range(2):
                    p = fill(pe, "s", u, c)
                    q = (qT, QZ)[c][:, h, t * 128:(t + 1) * 128]
                    if t < 4:
                        mm(p[:, 0:NS], q, kT[:, h, 0:NS], start=True, stop=True)
                        filled(mm(p[:, NS:NS + PAST], q, kcT[:, h, :], start=True, stop=True), "s", u, c)
                    else:
                        filled(mm(p[:, 0:NP], q, kT[:, h, NS:], start=True, stop=True), "s", u, c)

            def turn(u):
                p = fill(pe, "aT", u)
                pe.wait_ge(sig("a_ready"), u + 1)
                for i in range(5 if UNITS[u][0] < 4 else 1):
                    ins = pe.transpose(p[:, i * 128:(i + 1) * 128], PR[:, u % 2, 0, i * 128:(i + 1) * 128], ident)
                filled(ins, "aT", u)

            def values(u):
                t, h = UNITS[u]
                p = fill(pe, "av", u)
                after(pe, "aT", u)
                hc = slice(h * 128, (h + 1) * 128)
                vs = [V[:, i, hc] for i in range(4)] + [VC[:, hc]] if t < 4 else [V[:, 4, hc]]
                for i, v in enumerate(vs):
                    ins = mm(p[:, 0:128], AT[:, u % 2, i * 128:(i + 1) * 128], v, start=(i == 0), stop=(i == len(vs) - 1))
                filled(ins, "av", u)

            pe.wait_ge(sig("queries_ready"), 1)
            after(pe, "kcT")
            after(pe, "v", NT - 1)
            NU = len(UNITS)
            for i in range(NU + 2):
                if i < NU:
                    scores(i)
                if 1 <= i <= NU:
                    turn(i - 1)
                if i in SUMS_AT_UNIT:
                    kind, l, c = SUMS_AT_UNIT[i]
                    (row_sums if kind == "row" else turned_sums)(l, c)
                if i >= 2:
                    values(i - 2)
            pe.wait_ge(sig("o_normed"), 1)
            for h in range(HEADS):
                p = fill(pe, "oT", h)
                for t in range(NT):
                    ins = pe.transpose(p[:, t * 128:(t + 1) * 128], OR[:, t, h * 128:(h + 1) * 128], ident)
                filled(ins, "oT", h)
            pe.wait_ge(sig("cat_u"), HC)
            for h in range(HEADS):
                after(pe, "oT", h)
            tail(0, "out_e", lambda k: catU[:, k, :] if k < 4 else oT[:, k - 4, :])
            ranks_and_table(0)
            experts(0)

            def pool_map(j):
                p = fill(pe, "pool", j)
                pe.wait_ge(sig("pooled"), j + 1)
                for cols in (slice(0, NS), slice(NS, TOK)):
                    ins = mm(p[:, cols], PW[:, j, :], DP[:, j % 2, cols], start=True, stop=True)
                filled(ins, "pool", j)

            first_norm(1)
            pe.wait_ge(sig("pool_w_loaded"), 16)
            wx = page(pe, ("in_o", 0))
            for j in range(HC):
                project(wx, j, "xc", j)
                if j:
                    pool_map(j - 1)
                for c in SUMS_AT["xc"][j]:
                    row_sums(1, c)
            page_used()
            wh, wc = page(pe, ("in_o", 1)), page(pe, ("in_o", 3))
            for j in range(HC):
                project(wh, j, "hd", j)
                project(wc, j, "cg", j)
                if j == 0:
                    pool_map(HC - 1)
                for c in SUMS_AT["cg"][j]:
                    row_sums(1, c)
            page_used(2)
            wb = page(pe, ("in_o", 2))
            for j in range(HC):
                project(wb, j, "bg", j)
                if j == HC - 1:
                    page_used()
                for c in SUMS_AT["bg"][j]:
                    row_sums(1, c)
            pe.wait_ge(sig("short_conv"), HC)
            after(pe, "pool", HC - 1)
            tail(1, "out_o", lambda k: CAT[:, k, :])
            ranks_and_table(1)
            experts(1)


_INS = ["x_prompt", "x_sample", "cache_k", "cache_v", "c", "c_ctx", "w_ada", "b_ada", "g_norm1", "g_norm2", "g_final",
        "w_in_e", "conv_a_w", "conv_a_b", "ln_a_g", "ln_a_b", "lam_q1", "lam_k1", "lam_q2", "lam_k2", "subln_g", "w_out_e",
        "w_in_o", "pool_w", "pool_scale", "conv_d_w", "w_out_o", "w_router_g", "b_router_g", "w_router_e", "b_router_e",
        "w_gate", "w_up", "w_down"]
_OUTS = [("y_prompt", (1, 128, 1024)), ("y_sample", (1, 512, 1024)), ("new_cache_k", (1, 1, 128, 4, 2, 64)),
         ("new_cache_v", (1, 1, 128, 4, 128))]


def kernel(**inputs):
    import concourse.bacc as bacc
    from concourse.bass_utils import run_bass_kernel_spmd

    nc = bacc.Bacc("TRN2", target_bir_lowering=False, num_devices=1)
    arrays, aps = {}, {}
    for name, value in [(n, inputs[n]) for n in _INS] + list(shape_constants().items()):
        value = np.ascontiguousarray(value)
        arrays[name] = value
        aps[name] = nc.dram_tensor(name, value.shape, mybir.dt.from_np(value.dtype), kind="ExternalInput").ap()
    outs = {n: nc.dram_tensor(n, s, mybir.dt.float32, kind="ExternalOutput").ap() for n, s in _OUTS}
    build(nc, aps, outs)
    r = run_bass_kernel_spmd(nc, [arrays], core_ids=[0])
    return tuple(r.results[0][n] for n, _ in _OUTS)
```
